# Optimizing a Trainium2 kernel written in Bass

```python
import math
import jax
import jax.numpy as jnp
from jax import lax
import numpy as np

D_MODEL = 1024
BATCH = 1
SEQ = 256
DEPTH = 2

ATTN_HEADS = 8
HEAD_DIM = 64
ATTN_WIDTH = ATTN_HEADS * HEAD_DIM
CONV_WIDTH = D_MODEL - ATTN_WIDTH
CONV_K = 3
ROPE_DIM = HEAD_DIM // 4
ROPE_THETA = 500000.0
DILATED_PAIRS = ((128, 1), (512, 4), (2048, 16))
SSM_GROUP = 16
SSM_GROUPS = D_MODEL // SSM_GROUP
SSM_STATE = 64
D_FF = ((8 * D_MODEL // 3 + 255) // 256) * 256
N_EXPERTS = 8
TOP_K = 2
D_FF_EXPERT = 7 * D_MODEL // 2
RMS_EPS = 1e-6
N_EVEN = (DEPTH + 1) // 2
N_ODD = DEPTH // 2
EVEN_SPLITS = (ATTN_WIDTH, 2 * ATTN_WIDTH, 3 * ATTN_WIDTH,
               3 * ATTN_WIDTH + CONV_WIDTH, 3 * ATTN_WIDTH + 2 * CONV_WIDTH)

kernel_name = 'hybrid_dilated_conv_s5_moe_trunk'

def _rmsnorm_f32(x, g):
    xf = x.astype(jnp.float32)
    return xf * lax.rsqrt(jnp.mean(xf * xf, axis=-1, keepdims=True) + RMS_EPS) * g.astype(jnp.float32)

def _ada_norm(x, g, shift, scale):
    y = _rmsnorm_f32(x, g) * (1.0 + scale[:, None, :].astype(jnp.float32)) + shift[:, None, :].astype(jnp.float32)
    return y.astype(x.dtype)

def _rope_tables(positions, dtype):
    inv = ROPE_THETA ** (-jnp.arange(0, ROPE_DIM, 2, dtype=jnp.float32) / ROPE_DIM)
    ang = positions.astype(jnp.float32)[..., None] * inv
    return jnp.cos(ang)[:, :, None, :].astype(dtype), jnp.sin(ang)[:, :, None, :].astype(dtype)

def _partial_rope(t, cos, sin):
    half = ROPE_DIM // 2
    t1 = t[..., :half]
    t2 = t[..., half:ROPE_DIM]
    return jnp.concatenate([t1 * cos - t2 * sin, t2 * cos + t1 * sin, t[..., ROPE_DIM:]], axis=-1)

def _dilated_branch(q, k, v, window, dil):
    bsz, seq, nh, hd = q.shape
    blk = window // dil
    span = blk * dil
    s_pad = -(-seq // span) * span
    nb = s_pad // span

    def to_blocks(t):
        t = jnp.pad(t, ((0, 0), (0, s_pad - seq), (0, 0), (0, 0)))
        return t.reshape(bsz, nb, blk, dil, nh, hd)

    def with_prev(t):
        prev = jnp.pad(t[:, :-1], ((0, 0), (1, 0), (0, 0), (0, 0), (0, 0), (0, 0)))
        return jnp.concatenate([prev, t], axis=2)

    qb = to_blocks(q)
    kc = with_prev(to_blocks(k))
    vc = with_prev(to_blocks(v)).astype(jnp.float32)
    s = jnp.einsum('bnqrhe,bnkrhe->bnrhqk', qb, kc).astype(jnp.float32)
    qi = jnp.arange(blk)[:, None]
    kj = jnp.arange(2 * blk)[None, :]
    dist = blk + qi - kj
    band = (dist >= 0) & (dist <= window // dil)
    has_prev = (jnp.arange(nb)[:, None, None] > 0) | (kj[None] >= blk)
    mask = band[None] & has_prev
    s = jnp.where(mask[:, None, None], s, -jnp.inf)
    m = jnp.max(s, axis=-1, keepdims=True)
    p = jnp.exp(s - m)
    l = jnp.sum(p, axis=-1)
    o = jnp.einsum('bnrhqk,bnkrhe->bnqrhe', p, vc)
    l_t = jnp.transpose(l, (0, 1, 4, 2, 3))
    lse = jnp.transpose(m[..., 0], (0, 1, 4, 2, 3)) + jnp.log(l_t)
    o = (o / l_t[..., None]).reshape(bsz, s_pad, nh, hd)[:, :seq]
    lse = lse.reshape(bsz, s_pad, nh)[:, :seq]
    return o, lse

def _even_mixer(h, cos, sin, w_in, conv_w, w_out):
    bsz, seq, _ = h.shape
    proj = h @ w_in
    q, k, v, b_gate, c_gate, xin = jnp.split(proj, EVEN_SPLITS, axis=-1)
    q = _partial_rope(q.reshape(bsz, seq, ATTN_HEADS, HEAD_DIM), cos, sin) * (HEAD_DIM ** -0.5)
    k = _partial_rope(k.reshape(bsz, seq, ATTN_HEADS, HEAD_DIM), cos, sin)
    v = v.reshape(bsz, seq, ATTN_HEADS, HEAD_DIM)
    outs, lses = zip(*[_dilated_branch(q, k, v, w, d) for (w, d) in DILATED_PAIRS])
    wts = jax.nn.softmax(jnp.stack(lses, axis=0), axis=0)
    a_out = jnp.sum(wts[..., None] * jnp.stack(outs, axis=0), axis=0)
    a_out = a_out.astype(h.dtype).reshape(bsz, seq, ATTN_WIDTH)
    u = c_gate * xin
    conv = lax.conv_general_dilated(u, conv_w[:, None, :], window_strides=(1,),
                                    padding=((CONV_K - 1, 0),),
                                    dimension_numbers=('NWC', 'WIO', 'NWC'),
                                    feature_group_count=CONV_WIDTH)
    b_out = b_gate * conv
    return jnp.concatenate([a_out, b_out], axis=-1) @ w_out

def _diag_scan(a_re, a_im, b_re, b_im):
    def combine(left, right):
        ar_l, ai_l, br_l, bi_l = left
        ar_r, ai_r, br_r, bi_r = right
        return (ar_r * ar_l - ai_r * ai_l,
                ar_r * ai_l + ai_r * ar_l,
                ar_r * br_l - ai_r * bi_l + br_r,
                ar_r * bi_l + ai_r * br_l + bi_r)
    _, _, x_re, x_im = lax.associative_scan(combine, (a_re, a_im, b_re, b_im), axis=0)
    return x_re, x_im

def _s5_mixer(h, a_re, a_im, log_step, b_re, b_im, c_re, c_im, d_skip, glu_w, glu_b):
    bsz, seq, d = h.shape
    f32 = jnp.float32
    hf = h.astype(f32)
    u = hf.reshape(bsz, seq, SSM_GROUPS, SSM_GROUP)
    a_re = a_re.astype(f32)
    a_im = a_im.astype(f32)
    dt = jnp.exp(log_step.astype(f32))[:, None]
    mag = jnp.exp(a_re * dt)
    abar_re = mag * jnp.cos(a_im * dt)
    abar_im = mag * jnp.sin(a_im * dt)
    den = a_re * a_re + a_im * a_im
    nr = abar_re - 1.0
    f_re = (nr * a_re + abar_im * a_im) / den
    f_im = (abar_im * a_re - nr * a_im) / den
    b_re = b_re.astype(f32)
    b_im = b_im.astype(f32)
    bb_re = f_re[..., None] * b_re - f_im[..., None] * b_im
    bb_im = f_re[..., None] * b_im + f_im[..., None] * b_re
    bu_re = jnp.einsum('gpc,bsgc->bsgp', bb_re, u)
    bu_im = jnp.einsum('gpc,bsgc->bsgp', bb_im, u)
    a_seq_re = jnp.broadcast_to(abar_re, (seq, SSM_GROUPS, SSM_STATE))
    a_seq_im = jnp.broadcast_to(abar_im, (seq, SSM_GROUPS, SSM_STATE))
    x_re, x_im = jax.vmap(_diag_scan, in_axes=(None, None, 0, 0))(a_seq_re, a_seq_im, bu_re, bu_im)
    y = (jnp.einsum('gcp,bsgp->bsgc', c_re.astype(f32), x_re)
         - jnp.einsum('gcp,bsgp->bsgc', c_im.astype(f32), x_im))
    y = y.reshape(bsz, seq, d) + d_skip.astype(f32) * hf
    g = jax.nn.gelu(y).astype(h.dtype)
    val, gate = jnp.split(g @ glu_w + glu_b, 2, axis=-1)
    return val * jax.nn.sigmoid(gate)

def _swiglu(h, w_gate, w_up, w_down):
    return (jax.nn.silu(h @ w_gate) * (h @ w_up)) @ w_down

def _moe_swiglu(h, router_w, router_b, w_gate, w_up, w_down):
    bsz, seq, d = h.shape
    hf = h.reshape(bsz * seq, d)
    logits = (hf @ router_w + router_b).astype(jnp.float32)
    probs = jax.nn.softmax(logits, axis=-1)
    top_p, top_i = lax.top_k(probs, TOP_K)
    top_p = top_p / jnp.sum(top_p, axis=-1, keepdims=True)
    gates = jnp.sum(jax.nn.one_hot(top_i, N_EXPERTS, dtype=jnp.float32) * top_p[..., None], axis=1)
    gates = gates.astype(h.dtype)
    out = jnp.zeros_like(hf)
    for e in range(N_EXPERTS):
        out = out + gates[:, e:e + 1] * _swiglu(hf, w_gate[e], w_up[e], w_down[e])
    return out.reshape(bsz, seq, d)

def setup_inputs(seed: int = 0) -> dict:
    key = jax.random.key(seed)
    ks = jax.random.split(key, 32)
    f32 = jnp.float32
    D = D_MODEL

    def nrm(k, shape, scale):
        return jax.random.normal(k, shape, f32) * scale

    x = nrm(ks[0], (BATCH, SEQ, D), 1.0)
    c = nrm(ks[1], (BATCH, D), 1.0)
    offs = jax.random.randint(ks[2], (BATCH, 1), 0, 1024, dtype=jnp.int32)
    positions = offs + jnp.arange(SEQ, dtype=jnp.int32)[None, :]
    mod_w = nrm(ks[3], (DEPTH, D, 6 * D), D ** -0.5)
    mod_b = nrm(ks[4], (DEPTH, 6 * D), 0.02)
    norm_mix_g = 1.0 + nrm(ks[5], (DEPTH, D), 0.02)
    norm_ffn_g = 1.0 + nrm(ks[6], (DEPTH, D), 0.02)
    ev_w_in = nrm(ks[7], (N_EVEN, D, 3 * ATTN_WIDTH + 3 * CONV_WIDTH), D ** -0.5)
    ev_conv_w = nrm(ks[8], (N_EVEN, CONV_K, CONV_WIDTH), CONV_K ** -0.5)
    ev_w_out = nrm(ks[9], (N_EVEN, D, D), D ** -0.5)
    ffn_w_gate = nrm(ks[10], (N_EVEN, D, D_FF), D ** -0.5)
    ffn_w_up = nrm(ks[11], (N_EVEN, D, D_FF), D ** -0.5)
    ffn_w_down = nrm(ks[12], (N_EVEN, D_FF, D), D_FF ** -0.5)
    n_idx = jnp.arange(SSM_STATE, dtype=f32)
    ssm_a_re = -0.5 + nrm(ks[13], (N_ODD, SSM_GROUPS, SSM_STATE), 0.01)
    ssm_a_im = math.pi * n_idx + nrm(ks[14], (N_ODD, SSM_GROUPS, SSM_STATE), 0.01)
    ssm_log_step = jax.random.uniform(ks[15], (N_ODD, SSM_GROUPS), f32, math.log(1e-3), math.log(1e-1))
    ssm_b_re = nrm(ks[16], (N_ODD, SSM_GROUPS, SSM_STATE, SSM_GROUP), (2 * SSM_GROUP) ** -0.5)
    ssm_b_im = nrm(ks[17], (N_ODD, SSM_GROUPS, SSM_STATE, SSM_GROUP), (2 * SSM_GROUP) ** -0.5)
    ssm_c_re = nrm(ks[18], (N_ODD, SSM_GROUPS, SSM_GROUP, SSM_STATE), SSM_STATE ** -0.5)
    ssm_c_im = nrm(ks[19], (N_ODD, SSM_GROUPS, SSM_GROUP, SSM_STATE), SSM_STATE ** -0.5)
    ssm_d = nrm(ks[20], (N_ODD, D), 1.0)
    glu_w = nrm(ks[21], (N_ODD, D, 2 * D), D ** -0.5)
    glu_b = nrm(ks[22], (N_ODD, 2 * D), 0.02)
    moe_router_w = nrm(ks[23], (N_ODD, D, N_EXPERTS), D ** -0.5)
    moe_router_b = nrm(ks[24], (N_ODD, N_EXPERTS), 0.01)
    moe_w_gate = nrm(ks[25], (N_ODD, N_EXPERTS, D, D_FF_EXPERT), D ** -0.5)
    moe_w_up = nrm(ks[26], (N_ODD, N_EXPERTS, D, D_FF_EXPERT), D ** -0.5)
    moe_w_down = nrm(ks[27], (N_ODD, N_EXPERTS, D_FF_EXPERT, D), D_FF_EXPERT ** -0.5)
    final_norm_g = 1.0 + nrm(ks[28], (D,), 0.02)
    return {'x': x, 'c': c, 'positions': positions, 'mod_w': mod_w, 'mod_b': mod_b,
            'norm_mix_g': norm_mix_g, 'norm_ffn_g': norm_ffn_g,
            'ev_w_in': ev_w_in, 'ev_conv_w': ev_conv_w, 'ev_w_out': ev_w_out,
            'ffn_w_gate': ffn_w_gate, 'ffn_w_up': ffn_w_up, 'ffn_w_down': ffn_w_down,
            'ssm_a_re': ssm_a_re, 'ssm_a_im': ssm_a_im, 'ssm_log_step': ssm_log_step,
            'ssm_b_re': ssm_b_re, 'ssm_b_im': ssm_b_im, 'ssm_c_re': ssm_c_re, 'ssm_c_im': ssm_c_im,
            'ssm_d': ssm_d, 'glu_w': glu_w, 'glu_b': glu_b,
            'moe_router_w': moe_router_w, 'moe_router_b': moe_router_b,
            'moe_w_gate': moe_w_gate, 'moe_w_up': moe_w_up, 'moe_w_down': moe_w_down,
            'final_norm_g': final_norm_g}

def reference(x, c, positions, mod_w, mod_b, norm_mix_g, norm_ffn_g,
              ev_w_in, ev_conv_w, ev_w_out, ffn_w_gate, ffn_w_up, ffn_w_down,
              ssm_a_re, ssm_a_im, ssm_log_step, ssm_b_re, ssm_b_im, ssm_c_re, ssm_c_im,
              ssm_d, glu_w, glu_b, moe_router_w, moe_router_b,
              moe_w_gate, moe_w_up, moe_w_down, final_norm_g):
    cos, sin = _rope_tables(positions, x.dtype)
    cond = jax.nn.silu(c)
    for layer in range(DEPTH):
        mod = cond @ mod_w[layer] + mod_b[layer]
        sh_m, sc_m, g_m, sh_f, sc_f, g_f = jnp.split(mod, 6, axis=-1)
        i = layer // 2
        h = _ada_norm(x, norm_mix_g[layer], sh_m, sc_m)
        if layer % 2 == 0:
            mix = _even_mixer(h, cos, sin, ev_w_in[i], ev_conv_w[i], ev_w_out[i])
        else:
            mix = _s5_mixer(h, ssm_a_re[i], ssm_a_im[i], ssm_log_step[i], ssm_b_re[i], ssm_b_im[i],
                            ssm_c_re[i], ssm_c_im[i], ssm_d[i], glu_w[i], glu_b[i])
        x = x + g_m[:, None, :] * mix
        h = _ada_norm(x, norm_ffn_g[layer], sh_f, sc_f)
        if layer % 2 == 0:
            ff = _swiglu(h, ffn_w_gate[i], ffn_w_up[i], ffn_w_down[i])
        else:
            ff = _moe_swiglu(h, moe_router_w[i], moe_router_b[i], moe_w_gate[i], moe_w_up[i], moe_w_down[i])
        x = x + g_f[:, None, :] * ff
    return _rmsnorm_f32(x, final_norm_g).astype(x.dtype)


_drawn_inputs = setup_inputs


def setup_inputs(seed=0):
    import zlib

    import numpy as np

    out = dict(_drawn_inputs(seed))
    spreads = {}
    factors = {'ssm_a_re': 8.0,
     'ssm_b_im': 3.741,
     'ssm_c_re': 2.792,
     'ssm_c_im': 2.976,
     'glu_b': 8.0,
     'moe_router_b': 2.781,
     'final_norm_g': 2.742}
    for name, (base, spread) in spreads.items():
        noise = np.random.default_rng([zlib.crc32(name.encode()), seed]).standard_normal(out[name].shape)
        drawn = base * np.exp(spread * noise) if base else spread * noise
        out[name] = jnp.asarray(drawn.astype(out[name].dtype))
    for name, factor in factors.items():
        out[name] = (out[name] * factor).astype(out[name].dtype)
    return out
```

```python
from contextlib import ExitStack

import numpy as np

import concourse.bass as bass
from concourse import mybir

ALU = mybir.AluOpType
ACT = mybir.ActivationFunctionType
AX = mybir.AxisListType
F32 = mybir.dt.float32
I32 = mybir.dt.int32

P = 128
D = 1024
T = 256
NC = D // P
EPS = 1e-6
HEADS, HEAD = 8, 64
D_FF = 2816
D_FFE = 3584
EXPERTS = 8
FB = 256
FF_UNITS = D_FF // FB
EX_UNITS = D_FFE // FB
SLOT = 128
EXTRA = (2 * T) // (SLOT + 1)
assert T <= 2 * SLOT

GROUPS, GCH, STATES = 64, 16, 64
LB = P // GCH
KB = T // LB
TILES = GROUPS * STATES // P
BATCHES = 4
BT = TILES // BATCHES

RING = 14
PIECE = 2048
MOD_A, W_IN, MOD_B, W_OUT, MOD_C, FFN, SSM, GLU = 8, 12, 16, 4, 24, 3 * FF_UNITS, 3 * BATCHES, 8
DENSE = MOD_A + W_IN + MOD_B + W_OUT + MOD_C + FFN
PRE = DENSE + SSM + GLU
PER_ITEM = 3 * EX_UNITS
assert PER_ITEM % RING == 0

C_ID, C_ROT, C_ONE, C_TRI, C_BIAS, C_IOTA, C_REV, C_INV = 0, 240, 368, 496, 624, 1008, 1136, 1152
C_EPS, C_QUAD = 1153, 1154
C_ALL = 1155
K_C, K_MODB, K_GAIN, K_CONV, K_D, K_GLUB, K_ARE, K_AIM, K_LS, K_RB, K_RW = 0, 8, 104, 144, 156, 164, 180, 212, 244, 276, 292
K_ALL = 356

MAGIC = 12582912.0
PI_LOW = 3.1415925


def two_pi_parts():
    full = 2 * np.pi
    first = 6.28125
    second = float(np.float32(np.round((full - first) * 2 ** 20) / 2 ** 20))
    return first, second, float(np.float32(full - first - second))


def unit_order(units):
    order = []
    for f in range(units):
        order += [("gate", f), ("up", f)]
        if f:
            order.append(("down", f - 1))
    return order + [("down", units - 1)]


def unit_index(units):
    return {key: n for n, key in enumerate(unit_order(units))}


def trunk_kernel(nc, xt_in, pos_in, cols_in, consts_in, ssm_in, dense_in, expert_in, h_scr, y_scr, ssm_scr, out):
    ctx = ExitStack()
    with ctx:
        def sb(name, cols, dt=F32):
            return ctx.enter_context(nc.sbuf_tensor(name, [P, cols], dt))

        def sem(name):
            return ctx.enter_context(nc.semaphore(name))

        PS = ctx.enter_context(nc.psum_tensor("PS", [P, 8, 512], F32))
        ring = sb("ring", RING * PIECE)
        buf_a = sb("buf_a", NC * T)
        buf_b = sb("buf_b", NC * T)
        buf_h = sb("buf_h", NC * T)
        consts = sb("consts", C_ALL)
        cols = sb("cols", K_ALL)
        ssm_par = sb("ssm_par", 4 * TILES * GCH)
        bb = sb("bb", 2 * TILES * GCH)
        pows = sb("pows", 4 * TILES * LB)
        phasor = sb("phasor", 2 * TILES * KB)
        work = sb("work", 10240)
        modc = sb("modc", 96)
        acol = sb("acol", 4 * NC)
        stat = sb("stat", T)
        items = sb("items", 4, I32)
        m8 = sb("m8", TILES)

        def chunked(b):
            return b[:, :].rearrange("p (c t) -> p c t", c=NC)

        A, B, H = chunked(buf_a), chunked(buf_b), chunked(buf_h)

        def resid(k):
            return A if k < 2 else B

        def scratch(k):
            return B if k < 2 else A

        ident = consts[:, C_ID:C_ID + P]
        rot = consts[:, C_ROT:C_ROT + P]
        ones = consts[:, C_ONE:C_ONE + P]
        tri = consts[:, C_TRI:C_TRI + P]
        att_bias = consts[:, C_BIAS:C_BIAS + 384]
        iota = consts[:, C_IOTA:C_IOTA + P]
        rev = consts[:, C_REV:C_REV + 16]

        o = 0

        def take(n):
            nonlocal o
            o += n
            assert o <= 10240
            return work[:, o - n:o]

        qT, kT, vT, bg = take(1024), take(1024), take(1024), take(1024)
        ub = take(4 * (T + 2)).rearrange("p (c t) -> p c t", c=4)
        sco, ptb = take(768), take(768)
        cosF, rtmp = take(288), take(512)
        sinF = take(288)
        ang, ang_k, sin_h = take(288), take(288), take(288)
        att_st = take(64)
        cond32 = take(NC * 32)
        mod_row = take(512)
        posi = take(T).bitcast(I32)
        s_cols = [take(TILES) for _ in range(15)]
        o = 0
        bsm, bt_out, ct_out, t_out = take(2048), take(2048), take(2048), take(2048)
        f_act, f_hid = take(512), take(1024)
        cz, kc = take(512), stat[:, :]
        o = 0
        ust, vbuf, zbuf, xz = take(2048), take(2048), take(2048), take(4096)
        y_sb = vbuf
        gT = zbuf.rearrange("p (c t) -> p c t", c=NC)
        sig = ust
        o = 0
        h_tm, hgT = take(2048), take(1024)
        e_act_b, e_hid_b, sel, selg, gt, ye = take(256), take(512), take(256), take(256), take(256), take(1024)
        posx, gx = take(24), take(24)
        r = [take(16) for _ in range(12)]
        r2 = [take(2) for _ in range(8)]

        mod_bT = cols[:, K_MODB:K_MODB + 96]

        def gain(k):
            return cols[:, K_GAIN + 8 * k:K_GAIN + 8 * k + 8]

        def part(k, which):
            at = 48 * (k // 2) + 24 * (k % 2) + 8 * which
            return modc[:, at:at + 8]

        ssm = [ssm_par[:, i * 512:(i + 1) * 512].rearrange("p (t c) -> p t c", c=GCH) for i in range(4)]
        b_re, b_im, c_re, c_im = ssm
        bb_re, bb_im = [bb[:, i * 512:(i + 1) * 512].rearrange("p (t c) -> p t c", c=GCH) for i in range(2)]
        rp_re, rp_im, fp_re, fp_im = [pows[:, i * 256:(i + 1) * 256].rearrange("p (t b) -> p t b", b=LB)
                                      for i in range(4)]
        ph_re, ph_im = [phasor[:, i * 1024:(i + 1) * 1024].rearrange("p (t k) -> p t k", k=KB) for i in range(2)]

        ring_full = [sem(f"ring_full{s}") for s in range(RING)]
        row_evac, mod_cols = sem("row_evac"), sem("mod_cols")
        piece_done = sem("piece_done")
        (cols_loaded, x_loaded, tables_loaded, ssm_loaded, dve_step,) = [sem(n) for n in "cols_loaded x_loaded tables_loaded ssm_loaded dve_step".split()]
        (act_step, pool_step, cond_exp, cond_ready, dt_ready,) = [sem(n) for n in "act_step pool_step cond_exp cond_ready dt_ready".split()]
        (decay_arg, mag_ready, angle_ready, sines_ready, powers_ready,) = [sem(n) for n in "decay_arg mag_ready angle_ready sines_ready powers_ready".split()]
        (reversed_ready, squares_ready, sumsq_ready, rms_ready, h_ready,) = [sem(n) for n in "reversed_ready squares_ready sumsq_ready rms_ready h_ready".split()]
        (x_updated, mod_taken, proj_act, proj_dve, rope_psum,) = [sem(n) for n in "x_updated mod_taken proj_act proj_dve rope_psum".split()]
        (rope_ready, u_padded, scores_ready, masked_ready, negmax_ready,) = [sem(n) for n in "rope_ready u_padded scores_ready masked_ready negmax_ready".split()]
        (exp_ready, probs_ready, pt_psum, pt_ready, pv_ready,) = [sem(n) for n in "exp_ready probs_ready pt_psum pt_ready pv_ready".split()]
        (attn_out, conv_out, gate_act, hid_ready, bsm_ready,) = [sem(n) for n in "attn_out conv_out gate_act hid_ready bsm_ready".split()]
        (ct_ready, cz_ready, param_psum, param_evac, bt_spilled,) = [sem(n) for n in "ct_ready cz_ready param_psum param_evac bt_spilled".split()]
        (ct_spilled, t_spilled, h_stored, u_loaded, v_ready,) = [sem(n) for n in "ct_spilled t_spilled h_stored u_loaded v_ready".split()]
        (z_im_ready, scan_ready, xs_re, xs_im, y_evac, xz_zeroed) = [sem(n) for n in "z_im_ready scan_ready xs_re xs_im y_evac xz_zeroed".split()]
        (y_stored, y_loaded, yd_ready, gelu_ready, sig_ready,) = [sem(n) for n in "y_stored y_loaded yd_ready gelu_ready sig_ready".split()]
        (logits_ready, htm_psum, htm_ready, picked_ready, gap_ready,) = [sem(n) for n in "logits_ready htm_psum htm_ready picked_ready gap_ready".split()]
        (pick_exp, pos_ready, items_ready, e_act, e_hid,) = [sem(n) for n in "pick_exp pos_ready items_ready e_act e_hid".split()]
        (e_sel, e_selg, e_gtp, e_gt, e_gather,) = [sem(n) for n in "e_sel e_selg e_gtp e_gt e_gather".split()]
        (e_hg, e_y, e_scat, e_x, final_ready,) = [sem(n) for n in "e_hg e_y e_scat e_x final_ready".split()]
        (out_stored,) = [sem(n) for n in "out_stored".split()]

        def slot(n):
            return ring[:, (n % RING) * PIECE:(n % RING + 1) * PIECE]

        def param_steps():
            at = {}
            for q in range(BATCHES):
                for s in range(5):
                    at.setdefault(5 + 7 * q + s, []).append((q, s))
            return at

        PSTEPS = param_steps()
        PUSE = [0, 2, 4, 5, 7]

        block = ctx.enter_context(nc.Block())

        @block.sync
        def _(sp):
            def load(n, src):
                if n >= RING:
                    sp.wait_ge(piece_done, n - RING + 1)
                sp.dma_start(slot(n), src).then_inc(ring_full[n % RING], 16)

            for n in range(DENSE):
                load(n, dense_in[n])
            sp.wait_ge(bt_spilled, 16 * BATCHES)
            sp.wait_ge(ct_spilled, 16 * BATCHES)
            sp.wait_ge(t_spilled, 16 * BATCHES)
            for n in range(SSM):
                load(DENSE + n, ssm_scr[n])
            for n in range(GLU):
                load(DENSE + SSM + n, dense_in[DENSE + n])

            def expert(e, item):
                for j in range(PER_ITEM):
                    n = PRE + j
                    sp.wait_ge(piece_done, item * PER_ITEM + (n - RING + 1))
                    sp.dma_start(slot(n), expert_in[bass.ds(e * PER_ITEM + j, 1)].rearrange("o p n -> (o p) n")).then_inc(
                        ring_full[n % RING], 16)

            with sp.Fori(0, EXPERTS) as e:
                expert(e, e)
            sp.wait_ge(items_ready, 1)
            count = sp.value_load(items[0:1, 0:1], min_val=EXPERTS, max_val=EXPERTS + EXTRA)
            for extra in range(EXTRA):
                with sp.If(count > EXPERTS + extra):
                    e = sp.value_load(items[0:1, 1 + extra:2 + extra], min_val=0, max_val=EXPERTS - 1)
                    expert(e, EXPERTS + extra)

        FFI, EXI = unit_index(FF_UNITS), unit_index(EX_UNITS)
        AT_QKV = MOD_A
        AT_MODB = AT_QKV + W_IN
        AT_WOUT = AT_MODB + MOD_B
        AT_MODC = AT_WOUT + W_OUT
        AT_FFN = AT_MODC + MOD_C
        AT_BT, AT_T, AT_CT = DENSE, DENSE + BATCHES, DENSE + 2 * BATCHES
        AT_GLU = DENSE + SSM

        @block.tensor
        def _(pe):
            used = [0]

            def piece():
                n = used[0]
                pe.wait_ge(ring_full[n % RING], 16 * (n // RING + 1))
                used[0] += 1
                return slot(n)

            def k_chunks(w):
                return w.rearrange("p (c n) -> p c n", c=NC)

            def sums(k, bank):
                for cp in range(4):
                    pe.wait_ge(squares_ready, 4 * k + cp + 1)
                    for c in (2 * cp, 2 * cp + 1):
                        mm = pe.matmul(PS[:, bank, 0:T], ones, scratch(k)[:, c, :], start=(c == 0), stop=(c == NC - 1))
                mm.then_inc(sumsq_ready, 1)

            groups = [0]

            def mod_rows():
                if groups[0]:
                    pe.wait_ge(row_evac, groups[0])
                for j in range(2):
                    w = k_chunks(piece())
                    for c in range(NC):
                        q = 32 * (c % 4)
                        mm = pe.matmul(PS[q:q + 32, 6, j * FB:(j + 1) * FB], cond32[:, 32 * c:32 * c + 32], w[:, c, :],
                                       start=(c < 4), stop=(c >= 4))
                    mm.then_inc(piece_done, 1)
                groups[0] += 1

            def mod_turn():
                g = groups[0]
                pe.wait_ge(row_evac, g)
                for m in range(4):
                    at = 4 * (g - 1) + m
                    mm = pe.matmul(PS[:, 7, at:at + 1], mod_row[:, m * P:(m + 1) * P], consts[:, C_QUAD:C_QUAD + 1],
                                   start=True, stop=True)
                mm.then_inc(mod_cols, 1)

            def dense(bank, moving, chunk_sem=None, chunk_base=0):
                w = k_chunks(piece())
                for j in range(2):
                    for c in range(NC):
                        if chunk_sem is not None and j == 0:
                            pe.wait_ge(chunk_sem, chunk_base + c + 1)
                        mm = pe.matmul(PS[:, bank, j * T:(j + 1) * T], w[:, c, j * P:(j + 1) * P], moving[:, c, :],
                                       start=(c == 0), stop=(c == NC - 1))
                mm.then_inc(piece_done, 1)

            pe.wait_ge(tables_loaded, 32)
            sums(0, 0)
            pe.wait_ge(cond_ready, 1)
            for _ in range(MOD_A // 2):
                mod_rows()
                mod_turn()

            def rope(s):
                pe.wait_ge(proj_act, s + 1)
                if s >= 2:
                    pe.wait_ge(rope_ready, s - 1)
                src = (qT, kT)[s // 2]
                pe.matmul(PS[:, 3 + s % 2, :], rot, src[:, (s % 2) * 512:(s % 2 + 1) * 512], start=True,
                          stop=True).then_inc(rope_psum, 1)

            for w in range(W_IN):
                if w >= 2:
                    if w - 2 in (8, 9):
                        pe.wait_ge(proj_dve, w - 9)
                    else:
                        pe.wait_ge(proj_act, w - 1)
                bank = 1 + w % 2
                if w in (4, 5):
                    wv = k_chunks(piece())
                    for tt in range(2):
                        for c in range(NC):
                            mm = pe.matmul(PS[:, bank, tt * T:(tt + 1) * T], H[:, c, tt * P:(tt + 1) * P], wv[:, c, :],
                                           start=(c == 0), stop=(c == NC - 1))
                    mm.then_inc(piece_done, 1)
                elif w == 0:
                    dense(bank, H, h_ready, 0)
                else:
                    dense(bank, H)
                if 1 <= w <= 4:
                    rope(w - 1)

            def score(h):
                pe.wait_ge(rope_ready, 4)
                if h >= 2:
                    pe.wait_ge(masked_ready, h - 1)
                r0, ch, bank = HEAD * (h % 2), (h // 2) * T, 3 + h % 2
                pe.matmul(PS[:, bank, 0:128], qT[r0:r0 + 64, ch:ch + 128], kT[r0:r0 + 64, ch:ch + 128],
                          start=True, stop=True)
                pe.matmul(PS[:, bank, 128:384], qT[r0:r0 + 64, ch + 128:ch + 256], kT[r0:r0 + 64, ch:ch + 256],
                          start=True, stop=True).then_inc(scores_ready, 1)

            def turn(h):
                pe.wait_ge(probs_ready, h + 1)
                if h >= 2:
                    pe.wait_ge(pt_ready, h - 1)
                s = sco[:, (h % 2) * 384:(h % 2 + 1) * 384]
                for i in range(3):
                    mm = pe.transpose(PS[:, (5, 0)[h % 2], i * P:(i + 1) * P], s[:, i * P:(i + 1) * P], ident)
                mm.then_inc(pt_psum, 1)

            def attend(h):
                pe.wait_ge(pt_ready, h + 1)
                if h // 2 >= 2:
                    pe.wait_ge(attn_out, h // 2 - 1)
                pt = ptb[:, (h % 2) * 384:(h % 2 + 1) * 384]
                r0, bank = HEAD * (h % 2), 1 + (h // 2) % 2
                pe.matmul(PS[r0:r0 + 64, bank, 0:256], vT[:, h * 64:(h + 1) * 64], pt[:, 0:256], start=True, stop=False,
                          skip_group_check=True)
                pe.matmul(PS[r0:r0 + 64, bank, 128:256], vT[:, 512 + h * 64:512 + (h + 1) * 64], pt[:, 256:384],
                          start=False, stop=True, skip_group_check=True).then_inc(pv_ready, 1)

            pe.wait_ge(proj_act, 10)
            pe.wait_ge(proj_dve, 2)
            score(0)
            score(1)
            for h in range(HEADS):
                if h:
                    mod_turn()
                mod_rows()
                turn(h)
                if h + 2 < HEADS:
                    score(h + 2)
                if h:
                    attend(h - 1)
            attend(HEADS - 1)
            mod_turn()

            pe.wait_ge(attn_out, 4)
            pe.wait_ge(conv_out, 4)
            for w in range(W_OUT):
                if w >= 2:
                    pe.wait_ge(x_updated, 2 * (w - 1))
                dense(3 + w % 2, H)

            sums(1, 2)
            pe.wait_ge(mod_taken, 2)
            for _ in range(MOD_C // 2):
                mod_rows()
                mod_turn()

            def param_bank(q, use):
                u = 9 * q + use
                if u >= 2:
                    pe.wait_ge(param_evac, u - 1)
                return 2 + u % 2

            def param_step(q, s):
                if s in (0, 1):
                    if s == 0:
                        pe.wait_ge(bsm_ready, q + 1)
                    for half in range(2):
                        bank = param_bank(q, PUSE[s] + half)
                        for i in range(4):
                            tile, ri = 4 * s + 2 * half + i // 2, i % 2
                            mm = pe.transpose(PS[:, bank, i * P:(i + 1) * P],
                                              bsm[:, ri * 1024 + tile * P:ri * 1024 + (tile + 1) * P], ident)
                        mm.then_inc(param_psum, 1)
                if s == 2:
                    pe.wait_ge(cz_ready, q + 1)
                    bank = param_bank(q, PUSE[s])
                    for tile in range(BT):
                        for ri in range(2):
                            mm = pe.matmul(PS[:, bank, tile * 32:(tile + 1) * 32],
                                           bsm[:, ri * 1024 + tile * P:ri * 1024 + (tile + 1) * P],
                                           cz[:, ri * 256 + tile * 32:ri * 256 + (tile + 1) * 32],
                                           start=(ri == 0), stop=(ri == 1))
                    mm.then_inc(param_psum, 1)
                if s in (3, 4):
                    pe.wait_ge(param_evac, 9 * q + 5)
                    for half in range(2):
                        bank = param_bank(q, PUSE[s] + half)
                        for i in range(2):
                            b = 4 * (s - 3) + 2 * half + i
                            off = C_ID + GCH * (LB - 1 - b)
                            mm = pe.matmul(PS[:, bank, i * 256:(i + 1) * 256], consts[:, off:off + P], kc,
                                           start=True, stop=True)
                        mm.then_inc(param_psum, 1)

            def segment(n):
                for q, s in PSTEPS.get(n, []):
                    param_step(q, s)

            def down(f):
                pe.wait_ge(hid_ready, f + 1)
                if f == 0:
                    pe.wait_ge(mod_taken, 3)
                w = piece()
                for j in range(2):
                    for n in range(NC):
                        mm = pe.matmul(PS[:, 4 + n // 2, (n % 2) * T:(n % 2 + 1) * T],
                                       w[:, j * D + n * P:j * D + (n + 1) * P],
                                       f_hid[:, (f % 2) * 512 + j * T:(f % 2) * 512 + (j + 1) * T],
                                       start=(f == 0 and j == 0 and n % 2 == 0), stop=(f == FF_UNITS - 1 and j == 1),
                                       skip_group_check=True)
                mm.then_inc(piece_done, 1)

            for f in range(FF_UNITS):
                if f:
                    pe.wait_ge(gate_act, f)
                    dense(0, H)
                else:
                    dense(0, H, h_ready, NC)
                segment(3 * f)
                if f:
                    pe.wait_ge(hid_ready, f)
                dense(1, H)
                segment(3 * f + 1)
                if f:
                    down(f - 1)
                    segment(3 * f + 2)
            down(FF_UNITS - 1)

            sums(2, 0)
            pe.wait_ge(u_loaded, 16 * LB)
            for q in range(BATCHES):
                w = piece().rearrange("p (t r m) -> p t r m", t=BT, r=2)
                for tl in range(BT):
                    tile = BT * q + tl
                    at = (tile % 16) * KB
                    for ri in range(2):
                        for half in range(2):
                            g = 2 * tile + half
                            mm = pe.matmul(PS[64 * half:64 * half + 64, 2 * ri + tile // 16, at:at + KB],
                                           w[:, tl, ri, 64 * half:64 * half + 64], ust[:, g * KB:(g + 1) * KB],
                                           start=True, stop=True)
                mm.then_inc(piece_done, 1)
            for q in range(BATCHES):
                w = piece().rearrange("p (g m) -> p g m", g=16)
                for gl in range(16):
                    g = 16 * q + gl
                    mm = pe.matmul(PS[:, 4 + q, gl * KB:(gl + 1) * KB], w[:, gl, :], ust[:, g * KB:(g + 1) * KB],
                                   start=(gl == 0), stop=False, skip_group_check=True)
                mm.then_inc(piece_done, 1)
            pe.wait_ge(xs_re, 2)
            pe.wait_ge(xs_im, 2)
            for q in range(BATCHES):
                w = piece().rearrange("p (t r m) -> p t r m", t=BT, r=2)
                for tl in range(BT):
                    tile = BT * q + tl
                    for ri in range(2):
                        mm = pe.matmul(PS[:, 4 + q, tl * 64:(tl + 1) * 64], w[:, tl, ri, :],
                                       xz[:, ri * 2048 + tile * 64:ri * 2048 + (tile + 1) * 64],
                                       start=False, stop=(ri == 1), skip_group_check=True)
                mm.then_inc(piece_done, 1)

            for i in range(4):
                if i >= 2:
                    pe.wait_ge(x_updated, 16 + 2 * (i - 1))
                if i == 0:
                    for cp in range(4):
                        pe.wait_ge(gelu_ready, cp + 1)
                dense(i % 2, gT)
                dense(2 + i % 2, gT)

            sums(3, 4)
            pe.wait_ge(h_ready, 4 * NC)
            for tt in range(2):
                for c in range(NC):
                    mm = pe.matmul(PS[:, 5, tt * 8:tt * 8 + 8], H[:, c, tt * P:(tt + 1) * P],
                                   cols[:, K_RW + 8 * c:K_RW + 8 * c + 8], start=(c == 0), stop=(c == NC - 1))
            mm.then_inc(logits_ready, 1)
            for m in range(4):
                for i in range(4):
                    tt, c = (4 * m + i) // NC, (4 * m + i) % NC
                    mm = pe.transpose(PS[:, (6, 7, 0, 1)[m], i * P:(i + 1) * P], H[:, c, tt * P:(tt + 1) * P], ident)
                mm.then_inc(htm_psum, 1)
            pe.wait_ge(picked_ready, 1)
            M = r[7]
            pe.matmul(PS[:, 2, 0:8], tri, M[:, 0:8], start=True, stop=True)
            pe.matmul(PS[:, 2, 8:16], tri, M[:, 8:16], start=True, stop=False)
            pe.matmul(PS[:, 2, 8:16], ones, M[:, 0:8], start=False, stop=True)
            pe.matmul(PS[:, 2, 16:24], ones, M[:, 0:8], start=True, stop=False)
            pe.matmul(PS[:, 2, 16:24], ones, M[:, 8:16], start=False, stop=True).then_inc(pos_ready, 1)

            def gather():
                for c in range(NC):
                    for tt in range(2):
                        mm = pe.matmul(PS[:, 6 + c // 4, (c % 4) * SLOT:(c % 4 + 1) * SLOT],
                                       h_tm[:, tt * D + c * P:tt * D + (c + 1) * P], sel[:, tt * SLOT:(tt + 1) * SLOT],
                                       start=(tt == 0), stop=(tt == 1))
                mm.then_inc(e_gather, 1)

            pe.wait_ge(htm_ready, 4)
            pe.wait_ge(e_sel, 1)
            gather()
            pe.wait_ge(items_ready, 1)
            count = pe.value_load(items[0:1, 0:1], min_val=EXPERTS, max_val=EXPERTS + EXTRA)
            with pe.Fori(0, count) as it:
                def e_piece(key):
                    n = PRE + EXI[key]
                    pe.wait_ge(ring_full[n % RING], it * (16 * PER_ITEM // RING) + 16 * (n // RING + 1))
                    return slot(n)

                def into(bank, w):
                    w = k_chunks(w)
                    for j in range(2):
                        for c in range(NC):
                            mm = pe.matmul(PS[:, bank, j * SLOT:(j + 1) * SLOT], w[:, c, j * P:(j + 1) * P],
                                           hgT[:, c * SLOT:(c + 1) * SLOT], start=(c == 0), stop=(c == NC - 1))
                    mm.then_inc(piece_done, 1)

                def e_down(f):
                    pe.wait_ge(e_hid, it * EX_UNITS + (f + 1))
                    w = e_piece(("down", f))
                    for j in range(2):
                        for n in range(2):
                            mm = pe.matmul(PS[:, 4 + n, :],
                                           e_hid_b[:, (f % 2) * 256 + j * SLOT:(f % 2) * 256 + (j + 1) * SLOT],
                                           w[:, j * D + n * 512:j * D + (n + 1) * 512],
                                           start=(f == 0 and j == 0), stop=(f == EX_UNITS - 1 and j == 1))
                    mm.then_inc(piece_done, 1)

                pe.wait_ge(e_hg, it + 1)
                for f in range(EX_UNITS):
                    if f:
                        pe.wait_ge(e_act, it * EX_UNITS + f)
                    into(0, e_piece(("gate", f)))
                    if f:
                        pe.wait_ge(e_hid, it * EX_UNITS + f)
                    into(1, e_piece(("up", f)))
                    if f == 1:
                        pe.wait_ge(e_selg, it + 1)
                        for tt in range(2):
                            mm = pe.transpose(PS[:, 2, tt * P:(tt + 1) * P], selg[:, tt * P:(tt + 1) * P], ident)
                        mm.then_inc(e_gtp, 1)
                    if f:
                        e_down(f - 1)
                pe.wait_ge(e_sel, it + 2)
                gather()
                e_down(EX_UNITS - 1)
                pe.wait_ge(e_y, it + 1)
                pe.wait_ge(e_gt, it + 1)
                pe.wait_ge(e_hg, it + 2)
                for m in range(4):
                    for j in range(2):
                        n = 2 * m + j
                        mm = pe.matmul(PS[:, (2, 3, 6, 7)[m], j * T:(j + 1) * T], ye[:, n * P:(n + 1) * P], gt,
                                       start=True, stop=True)
                    mm.then_inc(e_scat, 1)

            sums(4, 0)

        @block.scalar
        def _(act):
            steps = [0]

            def copy(out_ap, in_ap):
                return act.activation(out_ap, in_ap, ACT.Copy)

            act.dma_start(cols[:, :], cols_in).then_inc(cols_loaded, 16)
            act.dma_start(buf_a[:, :], xt_in).then_inc(x_loaded, 16)
            act.dma_start(consts[:, :], consts_in).then_inc(tables_loaded, 16)
            act.dma_start(posi, pos_in.partition_broadcast(P).rearrange("p o t -> p (o t)")).then_inc(tables_loaded, 16)
            act.dma_start(ssm_par[:, :], ssm_in).then_inc(ssm_loaded, 16)

            act.wait_ge(cols_loaded, 16)
            act.activation(att_st[:, 0:8], cols[:, K_C:K_C + 8], ACT.Exp, scale=-1.0).then_inc(cond_exp, 1)
            act.activation(s_cols[0], cols[:, K_LS:K_LS + 32], ACT.Exp).then_inc(dt_ready, 1)
            act.wait_ge(decay_arg, 1)
            act.activation(s_cols[2], s_cols[1], ACT.Exp).then_inc(mag_ready, 1)

            def take_rows(n, group):
                for g in range(group, group + n):
                    act.wait_ge(piece_done, (2 * g + 2) + (W_IN if g >= 4 else 0) + (W_OUT if g >= 12 else 0))
                    copy(mod_row, PS[:, 6, :]).then_inc(row_evac, 1)

            def squares(k, wait):
                for cp in range(4):
                    wait(cp)
                    act.activation(scratch(k)[:, 2 * cp:2 * cp + 2, :], resid(k)[:, 2 * cp:2 * cp + 2, :],
                                   ACT.Square).then_inc(squares_ready, 1)

            def root(k, bank):
                act.wait_ge(sumsq_ready, k + 1)
                act.activation(stat[:, :], PS[:, bank, 0:T], ACT.Sqrt, scale=1.0 / D,
                               bias=consts[:, C_EPS:C_EPS + 1]).then_inc(rms_ready, 1)

            def x_wait(k):
                return lambda cp: act.wait_ge(x_updated, 8 * (k - 1) + 2 * (cp + 1))

            act.wait_ge(x_loaded, 16)
            squares(0, lambda cp: None)
            act.wait_ge(angle_ready, 1)
            act.activation(sinF, ang, ACT.Sin).then_inc(sines_ready, 1)
            act.activation(sin_h, ang, ACT.Sin, scale=0.5).then_inc(sines_ready, 1)
            act.wait_ge(tables_loaded, 32)
            root(0, 0)
            take_rows(4, 0)

            for w in (0, 1, 2, 3, 4, 5, 6, 7, 10, 11):
                act.wait_ge(piece_done, AT_QKV + w + 1)
                src = PS[:, 1 + w % 2, :]
                if w < 4:
                    copy((qT, kT)[w // 2][:, (w % 2) * 512:(w % 2 + 1) * 512], src).then_inc(proj_act, 1)
                elif w < 6:
                    copy(vT.rearrange("p (t n) -> p t n", t=2)[:, :, (w - 4) * 256:(w - 3) * 256],
                         src.rearrange("p (t n) -> p t n", t=2)).then_inc(proj_act, 1)
                elif w < 8:
                    copy(ub[:, 2 * (w - 6):2 * (w - 6) + 2, 2:T + 2],
                         src.rearrange("p (c t) -> p c t", c=2)).then_inc(proj_act, 1)
                else:
                    copy(bg[:, (w - 10) * 512:(w - 9) * 512], src).then_inc(proj_act, 1)

            def exps(h):
                act.wait_ge(negmax_ready, h + 1)
                s = sco[:, (h % 2) * 384:(h % 2 + 1) * 384]
                nm = att_st[:, 16 + 2 * h:18 + 2 * h]
                l = att_st[:, 32 + 2 * h:34 + 2 * h]
                act.activation(s[:, 0:128], s[:, 0:128], ACT.Exp, bias=nm[:, 0:1], scale=0.125, accum_out=l[:, 0:1])
                act.activation(s[:, 128:384], s[:, 128:384], ACT.Exp, bias=nm[:, 1:2], scale=0.125,
                               accum_out=l[:, 1:2]).then_inc(exp_ready, 1)

            exps(0)
            for h in range(HEADS):
                if h + 1 < HEADS:
                    exps(h + 1)
                take_rows(1, 4 + h)
                act.wait_ge(pt_psum, h + 1)
                if h >= 2:
                    act.wait_ge(pv_ready, h - 1)
                copy(ptb[:, (h % 2) * 384:(h % 2 + 1) * 384], PS[:, (5, 0)[h % 2], 0:384]).then_inc(pt_ready, 1)

            squares(1, x_wait(1))
            root(1, 2)
            take_rows(12, 12)

            def param_take(q, use, out_ap, n, view=None):
                u = 9 * q + use
                act.wait_ge(param_psum, u + 1)
                src = PS[:, 2 + u % 2, 0:n]
                copy(out_ap, src if view is None else view(src)).then_inc(param_evac, 1)

            def param_step(q, s):
                if s in (0, 1):
                    if s == 0 and q:
                        act.wait_ge(bt_spilled, 16 * q)
                    for half in range(2):
                        at = (2 * s + half) * 512
                        param_take(q, PUSE[s] + half, bt_out[:, at:at + 512], 512)
                    if s == 1:
                        act.wait_ge(param_evac, 9 * q + 4)
                        act.dma_start(ssm_scr[q], bt_out).then_inc(bt_spilled, 16)
                if s == 2:
                    param_take(q, PUSE[s], kc, 256)
                    act.wait_ge(ct_ready, q + 1)
                    act.dma_start(ssm_scr[2 * BATCHES + q], ct_out).then_inc(ct_spilled, 16)
                if s in (3, 4):
                    if s == 3 and q:
                        act.wait_ge(t_spilled, 16 * q)
                    for half in range(2):
                        b = 4 * (s - 3) + 2 * half
                        dst = t_out.rearrange("p (g b c) -> p b g c", g=16, b=LB)[:, b:b + 2]
                        param_take(q, PUSE[s] + half, dst, 512,
                                   lambda a: a.rearrange("p (b g c) -> p b g c", b=2, g=16))
                    if s == 4:
                        act.wait_ge(param_evac, 9 * q + 9)
                        act.dma_start(ssm_scr[BATCHES + q], t_out).then_inc(t_spilled, 16)

            for f in range(FF_UNITS):
                act.wait_ge(piece_done, AT_FFN + FFI["gate", f] + 1)
                if f:
                    act.wait_ge(hid_ready, f)
                act.activation(f_act, PS[:, 0, :], ACT.Silu).then_inc(gate_act, 1)
                for n in (3 * f, 3 * f + 1, 3 * f + 2):
                    for q, s in PSTEPS.get(n, []):
                        param_step(q, s)

            squares(2, x_wait(2))
            root(2, 0)

            act.wait_ge(h_ready, 3 * NC)
            act.dma_start(h_scr.rearrange("(c p) t -> p c t", p=P), H).then_inc(h_stored, 16)
            act.wait_ge(h_stored, 16)
            for b in range(LB):
                act.dma_start(ust[GCH * b:GCH * (b + 1), :].rearrange("c (g k) -> c g k", g=GROUPS),
                              h_scr.rearrange("(g c) (b k) -> b c g k", c=GCH, b=LB)[b]).then_inc(u_loaded, 16)
            act.wait_ge(piece_done, AT_BT + BATCHES)
            copy(vbuf[:, 0:1024], PS[:, 0:2, :].rearrange("p b n -> p (b n)")).then_inc(v_ready, 1)
            copy(vbuf[:, 1024:2048], PS[:, 2:4, :].rearrange("p b n -> p (b n)")).then_inc(v_ready, 1)
            for q in range(BATCHES):
                act.wait_ge(piece_done, AT_CT + q + 1)
                copy(y_sb[:, q * 512:(q + 1) * 512], PS[:, 4 + q, :]).then_inc(y_evac, 1)
            act.wait_ge(y_evac, BATCHES)
            for b in range(LB):
                act.dma_start(y_scr.rearrange("(g c) (b k) -> b c g k", c=GCH, b=LB)[b],
                              y_sb[GCH * b:GCH * (b + 1), :].rearrange("c (g k) -> c g k", g=GROUPS)).then_inc(y_stored, 16)
            act.wait_ge(y_stored, 16 * LB)
            act.dma_start(A, y_scr.rearrange("(c p) t -> p c t", p=P)).then_inc(y_loaded, 16)
            for cp in range(4):
                act.wait_ge(yd_ready, 2 * (cp + 1))
                act.activation(gT[:, 2 * cp:2 * cp + 2, :], A[:, 2 * cp:2 * cp + 2, :], ACT.Gelu_apprx_tanh).then_inc(gelu_ready, 1)
            for i in range(4):
                act.wait_ge(piece_done, AT_GLU + 2 * i + 2)
                if i >= 2:
                    act.wait_ge(x_updated, 16 + 2 * (i - 1))
                for j in range(2):
                    at = (i % 2) * 512 + j * T
                    a = act.activation(sig[:, at:at + T], PS[:, 2 + i % 2, j * T:(j + 1) * T], ACT.Sigmoid,
                                       bias=cols[:, K_GLUB + 8 + 2 * i + j:K_GLUB + 9 + 2 * i + j])
                a.then_inc(sig_ready, 1)

            squares(3, x_wait(3))
            root(3, 4)

            for m in range(4):
                act.wait_ge(htm_psum, m + 1)
                copy(h_tm[:, m * 512:(m + 1) * 512], PS[:, (6, 7, 0, 1)[m], :]).then_inc(htm_ready, 1)
            act.wait_ge(gap_ready, 1)
            act.activation(r2[5], r2[4], ACT.Exp).then_inc(pick_exp, 1)

            def take_gathered():
                copy(hgT, PS[:, 6:8, :].rearrange("p b n -> p (b n)")).then_inc(e_hg, 1)

            act.wait_ge(e_gather, 1)
            take_gathered()
            act.wait_ge(items_ready, 1)
            count = act.value_load(items[0:1, 0:1], min_val=EXPERTS, max_val=EXPERTS + EXTRA)
            with act.Fori(0, count) as it:
                for f in range(EX_UNITS):
                    act.wait_ge(piece_done, it * PER_ITEM + (PRE + EXI["gate", f] + 1))
                    if f:
                        act.wait_ge(e_hid, it * EX_UNITS + f)
                    act.activation(e_act_b, PS[:, 0, 0:256], ACT.Silu).then_inc(e_act, 1)
                act.wait_ge(e_gather, it + 2)
                take_gathered()
                act.wait_ge(piece_done, it * PER_ITEM + (PRE + PER_ITEM))
                copy(ye, PS[:, 4:6, :].rearrange("p b n -> p (b n)")).then_inc(e_y, 1)
            act.wait_ge(e_x, count * 4)
            squares(4, lambda cp: None)
            root(4, 0)
            act.wait_ge(final_ready, NC)
            act.dma_start(out, buf_h[:, :]).then_inc(out_stored, 16)
            act.wait_ge(out_stored, 16)

        @block.vector
        def _(dve):
            steps = [0]

            def link(ins):
                steps[0] += 1
                ins.then_inc(dve_step, 1)
                dve.wait_ge(dve_step, steps[0])

            def tt(o_, a, b, op):
                return dve.tensor_tensor(o_, a, b, op)

            def cmul(o_re, o_im, a_re, a_im, b_re_, b_im_, tmp):
                tt(o_re, a_re, b_re_, ALU.mult)
                link(tt(tmp, a_im, b_im_, ALU.mult))
                link(tt(o_re, o_re, tmp, ALU.subtract))
                tt(o_im, a_re, b_im_, ALU.mult)
                link(tt(tmp, a_im, b_re_, ALU.mult))
                link(tt(o_im, o_im, tmp, ALU.add))

            dve.wait_ge(cond_exp, 1)
            link(dve.tensor_scalar(att_st[:, 8:16], att_st[:, 0:8], 1.0, None, ALU.add))
            link(dve.reciprocal(att_st[:, 8:16], att_st[:, 8:16]))
            tt(cond32.rearrange("p (c n) -> p c n", c=NC), att_st[:, 8:16].unsqueeze(2).broadcast_to([P, NC, 32]),
               cols[:, K_C:K_C + 8].unsqueeze(2).broadcast_to([P, NC, 32]), ALU.mult).then_inc(cond_ready, 1)
            dve.wait_ge(dt_ready, 1)
            are, aim = cols[:, K_ARE:K_ARE + 32], cols[:, K_AIM:K_AIM + 32]
            tt(s_cols[1], are, s_cols[0], ALU.mult).then_inc(decay_arg, 1)
            tt(ang[:, 256:288], aim, s_cols[0], ALU.mult)
            dve.wait_ge(tables_loaded, 32)
            link(dve.tensor_copy(ang[:, 0:T], posi))
            link(dve.tensor_scalar(ang[:, 0:T], ang[:, 0:T], consts[:, C_INV:C_INV + 1], None, ALU.mult))
            link(dve.tensor_scalar(ang_k, ang, 1.0 / (2 * np.pi), MAGIC, ALU.mult, ALU.add))
            link(dve.tensor_scalar(ang_k, ang_k, -MAGIC, None, ALU.add))
            for part_of in two_pi_parts():
                link(dve.scalar_tensor_tensor(ang, ang_k, -part_of, ang, ALU.mult, ALU.add))
            dve.tensor_scalar(ang, ang, PI_LOW, -PI_LOW, ALU.min, ALU.max).then_inc(angle_ready, 1)
            dve.wait_ge(sines_ready, 2)
            link(tt(cosF, sin_h, sin_h, ALU.mult))
            link(dve.tensor_scalar(cosF, cosF, -2.0, 1.0, ALU.mult, ALU.add))

            cos_a, sin_a = cosF[:, 256:288], sinF[:, 256:288]
            (dt_, _, mag, ab_re, ab_im, nr, den, t1, f_re, f_im, w_re, w_im, v_re, v_im) = s_cols[:14]
            dve.wait_ge(mag_ready, 1)
            tt(ab_re, mag, cos_a, ALU.mult)
            link(tt(ab_im, mag, sin_a, ALU.mult))
            dve.tensor_scalar(nr, ab_re, -1.0, None, ALU.add)
            tt(den, are, are, ALU.mult)
            link(tt(t1, aim, aim, ALU.mult))
            link(tt(den, den, t1, ALU.add))
            link(dve.reciprocal(den, den))
            tt(f_re, nr, are, ALU.mult)
            link(tt(t1, ab_im, aim, ALU.mult))
            link(tt(f_re, f_re, t1, ALU.add))
            tt(f_re, f_re, den, ALU.mult)
            tt(f_im, ab_im, are, ALU.mult)
            link(tt(t1, nr, aim, ALU.mult))
            link(tt(f_im, f_im, t1, ALU.subtract))
            link(tt(f_im, f_im, den, ALU.mult))

            def tmp3(n):
                return sco[:, 0:TILES * n].rearrange("p (t n) -> p t n", n=n)

            def wide(a, n):
                return a.unsqueeze(2).broadcast_to([P, TILES, n])

            dve.wait_ge(ssm_loaded, 16)
            cmul(bb_re, bb_im, wide(f_re, GCH), wide(f_im, GCH), b_re, b_im, tmp3(GCH))
            dve.tensor_copy(fp_re[:, :, 0], ab_re)
            link(dve.tensor_copy(fp_im[:, :, 0], ab_im))
            for n in (1, 2, 4):
                cmul(fp_re[:, :, n:2 * n], fp_im[:, :, n:2 * n], fp_re[:, :, 0:n], fp_im[:, :, 0:n],
                     wide(fp_re[:, :, n - 1], n), wide(fp_im[:, :, n - 1], n), tmp3(n))
            dve.tensor_copy(s_cols[14], aim).then_inc(powers_ready, 1)
            cmul(w_re, w_im, cos_a, sin_a, cos_a, sin_a, t1)
            cmul(v_re, v_im, w_re, w_im, w_re, w_im, t1)
            cmul(w_re, w_im, v_re, v_im, v_re, v_im, t1)
            dve.memset(ph_re[:, :, 0:1], 1.0)
            dve.memset(ph_im[:, :, 0:1], 0.0)
            dve.tensor_copy(ph_re[:, :, 1], w_re)
            link(dve.tensor_copy(ph_im[:, :, 1], w_im))
            ws = [(w_re, w_im), (v_re, v_im)]
            for lev, n in enumerate((2, 4, 8, 16)):
                (p_re, p_im), (q_re, q_im) = ws[lev % 2], ws[1 - lev % 2]
                cmul(q_re, q_im, p_re, p_im, p_re, p_im, t1)
                cmul(ph_re[:, :, n:2 * n], ph_im[:, :, n:2 * n], ph_re[:, :, 0:n], ph_im[:, :, 0:n],
                     wide(q_re, n), wide(q_im, n), tmp3(n))
            link(tt(m8[:, :], mag, mag, ALU.mult))
            link(tt(m8[:, :], m8[:, :], m8[:, :], ALU.mult))
            link(tt(m8[:, :], m8[:, :], m8[:, :], ALU.mult))

            def normalise(k):
                dve.wait_ge(rms_ready, k + 1)
                link(dve.reciprocal(stat[:, :], stat[:, :]))
                link(tt(scratch(k), resid(k), stat[:, :].unsqueeze(1).broadcast_to([P, NC, T]), ALU.mult))

            def modulate(k):
                a = acol[:, 8 * k:8 * k + 8]
                link(dve.tensor_scalar(a, part(k, 1), 1.0, None, ALU.add))
                link(tt(a, a, gain(k), ALU.mult))
                for c in range(NC):
                    dve.tensor_scalar(H[:, c, :], scratch(k)[:, c, :], a[:, c:c + 1], part(k, 0)[:, c:c + 1],
                                      ALU.mult, ALU.add).then_inc(h_ready, 1)

            def mod_take(n, to, group):
                dve.wait_ge(mod_cols, group)
                tt(modc[:, to:to + n], PS[:, 7, to:to + n], mod_bT[:, to:to + n], ALU.add).then_inc(mod_taken, 1)

            normalise(0)
            mod_take(16, 0, 4)
            dve.wait_ge(mod_taken, 1)
            modulate(0)

            def rope(s):
                dve.wait_ge(rope_psum, s + 1)
                if s:
                    dve.wait_ge(rope_ready, s)
                rows = (qT, kT)[s // 2][:, (s % 2) * 512:(s % 2 + 1) * 512].rearrange("p (c t) -> p c t", c=2)
                turned = rtmp.rearrange("p (c t) -> p c t", c=2)
                tt(turned, PS[:, 3 + s % 2, :].rearrange("p (c t) -> p c t", c=2),
                   sinF[:, 0:T].unsqueeze(1).broadcast_to([P, 2, T]), ALU.mult)
                link(tt(rows, rows, cosF[:, 0:T].unsqueeze(1).broadcast_to([P, 2, T]), ALU.mult))
                tt(rows, rows, turned, ALU.add).then_inc(rope_ready, 1)

            for s in range(4):
                rope(s)
            dve.wait_ge(u_padded, 1)
            for w in (8, 9):
                dve.wait_ge(piece_done, AT_QKV + w + 1)
                dve.wait_ge(proj_act, 7 + w - 8)
                rows = ub[:, 2 * (w - 8):2 * (w - 8) + 2, 2:T + 2]
                tt(rows, rows, PS[:, 1 + w % 2, :].rearrange("p (c t) -> p c t", c=2), ALU.mult).then_inc(proj_dve, 1)

            def mask(h):
                dve.wait_ge(scores_ready, h + 1)
                if h >= 2:
                    dve.wait_ge(pt_psum, h - 1)
                s = sco[:, (h % 2) * 384:(h % 2 + 1) * 384]
                bank = 3 + h % 2
                mx = att_st[:, 48 + 2 * (h % 2):50 + 2 * (h % 2)]
                link(tt(s, PS[:, bank, 0:384], att_bias, ALU.add))
                dve.tensor_reduce(mx[:, 0:1], s[:, 0:128], AX.X, ALU.max).then_inc(masked_ready, 1)
                link(dve.tensor_reduce(mx[:, 1:2], s[:, 128:384], AX.X, ALU.max))
                dve.tensor_scalar(att_st[:, 16 + 2 * h:18 + 2 * h], mx, -0.125, None, ALU.mult).then_inc(negmax_ready, 1)

            def scale(h):
                dve.wait_ge(exp_ready, h + 1)
                s = sco[:, (h % 2) * 384:(h % 2 + 1) * 384]
                l = att_st[:, 32 + 2 * h:34 + 2 * h]
                link(dve.reciprocal(l, l))
                dve.tensor_scalar(s[:, 0:128], s[:, 0:128], l[:, 0:1], None, ALU.mult)
                dve.tensor_scalar(s[:, 128:384], s[:, 128:384], l[:, 1:2], None, ALU.mult).then_inc(probs_ready, 1)

            def head_pair(j):
                dve.wait_ge(pv_ready, 2 * j + 2)
                dve.tensor_copy(H[:, j, :], PS[:, 1 + j % 2, 0:T]).then_inc(attn_out, 1)

            def conv(c):
                k0 = K_CONV + c
                if c == 0:
                    dve.wait_ge(proj_dve, 2)
                    dve.wait_ge(proj_act, 10)
                y = H[:, 4 + c, :]
                link(dve.tensor_scalar(y, ub[:, c, 0:T], cols[:, k0:k0 + 1], None, ALU.mult))
                link(dve.scalar_tensor_tensor(y, ub[:, c, 1:T + 1], cols[:, k0 + 4:k0 + 5], y, ALU.mult, ALU.add))
                link(dve.scalar_tensor_tensor(y, ub[:, c, 2:T + 2], cols[:, k0 + 8:k0 + 9], y, ALU.mult, ALU.add))
                tt(y, y, bg[:, c * T:(c + 1) * T], ALU.mult).then_inc(conv_out, 1)

            mask(0)
            for h in range(HEADS):
                if h + 1 < HEADS:
                    mask(h + 1)
                if h < 4:
                    conv(h)
                scale(h)
                if h >= 3 and h % 2:
                    head_pair((h - 3) // 2)
            head_pair(3)

            def residual(k, ch, src):
                return dve.scalar_tensor_tensor(resid(k)[:, ch, :], src, part(k, 2)[:, ch:ch + 1], resid(k)[:, ch, :],
                                                ALU.mult, ALU.add)

            mod_take(32, 16, 12)
            dve.wait_ge(mod_taken, 2)
            for w in range(W_OUT):
                dve.wait_ge(piece_done, AT_WOUT + w + 1)
                for j in range(2):
                    residual(0, 2 * w + j, PS[:, 3 + w % 2, j * T:(j + 1) * T]).then_inc(x_updated, 1)
            normalise(1)
            modulate(1)
            mod_take(48, 48, 24)

            def block_inputs(q):
                if q == 0:
                    dve.wait_ge(reversed_ready, 1)
                else:
                    dve.wait_ge(param_psum, 9 * (q - 1) + 5)
                ts = slice(BT * q, BT * (q + 1))

                def v4(a):
                    return a.rearrange("p (t b c) -> p t b c", t=BT, b=LB)

                o_re, o_im, tmp = v4(bsm[:, 0:1024]), v4(bsm[:, 1024:2048]), v4(buf_b[:, 0:1024])
                pr, pi = [a[:, ts, :].unsqueeze(3).broadcast_to([P, BT, LB, GCH]) for a in (rp_re, rp_im)]
                br, bi = [a[:, ts, :].unsqueeze(2).broadcast_to([P, BT, LB, GCH]) for a in (bb_re, bb_im)]
                tt(o_re, pr, br, ALU.mult)
                link(tt(tmp, pi, bi, ALU.mult))
                link(tt(o_re, o_re, tmp, ALU.subtract))
                tt(o_im, pr, bi, ALU.mult)
                link(tt(tmp, pi, br, ALU.mult))
                tt(o_im, o_im, tmp, ALU.add).then_inc(bsm_ready, 1)

            for f in range(FF_UNITS):
                dve.wait_ge(piece_done, AT_FFN + FFI["up", f] + 1)
                dve.wait_ge(gate_act, f + 1)
                if f >= 2:
                    dve.wait_ge(piece_done, AT_FFN + FFI["down", f - 2] + 1)
                tt(f_hid[:, (f % 2) * 512:(f % 2 + 1) * 512], f_act, PS[:, 1, :], ALU.mult).then_inc(hid_ready, 1)
                if f == 0:
                    block_inputs(0)
                for q in range(1, BATCHES):
                    if (5 + 7 * (q - 1) + 2) // 3 + 1 == f:
                        block_inputs(q)

            dve.wait_ge(piece_done, AT_FFN + 3 * FF_UNITS)
            dve.wait_ge(ct_ready, BATCHES)
            dve.wait_ge(bsm_ready, BATCHES)
            for n in range(NC):
                def blocked(a):
                    return a.rearrange("p (k b) -> p b k", b=LB)
                dve.scalar_tensor_tensor(B[:, n, :].rearrange("p (b k) -> p b k", b=LB),
                                         blocked(PS[:, 4 + n // 2, (n % 2) * T:(n % 2 + 1) * T]),
                                         part(1, 2)[:, n:n + 1], blocked(A[:, n, :]), ALU.mult, ALU.add).then_inc(x_updated, 1)
            dve.wait_ge(mod_taken, 3)
            normalise(2)
            modulate(2)

            dtab = pows[:, 0:1024].rearrange("p (t k) -> p t k", k=KB)
            link(dve.tensor_copy(dtab, wide(m8[:, :], KB)))
            link(dve.memset(dtab[:, :, 0:1], 0.0))
            flat_re, flat_im = phasor[:, 0:1024], phasor[:, 1024:2048]
            vr, vi, zr, zi = vbuf[:, 0:1024], vbuf[:, 1024:2048], zbuf[:, 0:1024], zbuf[:, 1024:2048]
            ta, xr = buf_a[:, 0:1024], buf_a[:, 1024:2048]
            dve.wait_ge(v_ready, 2)
            tt(zr, vr, flat_re, ALU.mult)
            link(tt(ta, vi, flat_im, ALU.mult))
            link(tt(zr, zr, ta, ALU.add))
            link(dve.tensor_tensor_scan(xr, pows[:, 0:1024], zr, 0.0, ALU.mult, ALU.add))
            dve.wait_ge(z_im_ready, 1)
            dve.tensor_tensor_scan(vr, pows[:, 0:1024], zi, 0.0, ALU.mult, ALU.add).then_inc(scan_ready, 1)
            dve.wait_ge(scan_ready, 1)
            tt(zr, xr, flat_re, ALU.mult)
            link(tt(ta, vr, flat_im, ALU.mult))
            dve.wait_ge(xz_zeroed, 1)
            x4 = xz.rearrange("p (r t g k) -> p r t g k", r=2, t=TILES, g=2)
            for g in range(2):
                rows = slice(64 * g, 64 * g + 64)
                tt(x4[rows, 0, :, g, 1:KB], zr.rearrange("p (t k) -> p t k", k=KB)[rows, :, 0:KB - 1],
                   ta.rearrange("p (t k) -> p t k", k=KB)[rows, :, 0:KB - 1], ALU.subtract).then_inc(xs_re, 1)

            dve.wait_ge(y_loaded, 16)
            for c in range(NC):
                dve.scalar_tensor_tensor(A[:, c, :], H[:, c, :], cols[:, K_D + c:K_D + c + 1], A[:, c, :],
                                         ALU.mult, ALU.add).then_inc(yd_ready, 1)
            for i in range(4):
                dve.wait_ge(piece_done, AT_GLU + 2 * i + 1)
                dve.wait_ge(sig_ready, i + 1)
                for j in range(2):
                    s = sig[:, (i % 2) * 512 + j * T:(i % 2) * 512 + (j + 1) * T]
                    bias = cols[:, K_GLUB + 2 * i + j:K_GLUB + 2 * i + j + 1]
                    link(dve.scalar_tensor_tensor(s, PS[:, i % 2, j * T:(j + 1) * T], bias, s, ALU.add, ALU.mult))
                    residual(2, 2 * i + j, s).then_inc(x_updated, 1)
            normalise(3)
            modulate(3)

            def v2(a):
                return a.rearrange("p (t e) -> p t e", e=EXPERTS)

            def wide2(a):
                return a.unsqueeze(2).broadcast_to([P, 2, EXPERTS])

            logit, eq, first, rest, second, gates, M, place = r[0], r[1], r[3], r[4], r[5], r[6], r[7], r[8]

            def best(src, onehot, mx, at):
                link(dve.tensor_reduce(mx, v2(src), AX.X, ALU.max))
                link(tt(v2(eq), v2(src), wide2(mx), ALU.is_equal))
                link(tt(eq, eq, rev, ALU.mult))
                link(dve.tensor_reduce(at, v2(eq), AX.X, ALU.max))
                link(tt(v2(onehot), v2(rev), wide2(at), ALU.is_equal))

            dve.wait_ge(logits_ready, 1)
            link(tt(logit, PS[:, 5, 0:16], cols[:, K_RB:K_RB + 16], ALU.add))
            best(logit, first, r2[0], r2[1])
            link(dve.scalar_tensor_tensor(rest, first, -3e38, logit, ALU.mult, ALU.add))
            best(rest, second, r2[2], r2[3])
            tt(M, first, second, ALU.add).then_inc(picked_ready, 1)
            tt(r2[4], r2[2], r2[0], ALU.subtract).then_inc(gap_ready, 1)
            dve.wait_ge(pick_exp, 1)
            link(dve.tensor_scalar(r2[6], r2[5], 1.0, None, ALU.add))
            link(dve.reciprocal(r2[6], r2[6]))
            link(tt(r2[7], r2[5], r2[6], ALU.mult))
            tt(v2(gates), v2(first), wide2(r2[6]), ALU.mult)
            link(tt(v2(eq), v2(second), wide2(r2[7]), ALU.mult))
            link(tt(gates, gates, eq, ALU.add))
            dve.wait_ge(pos_ready, 1)
            dve.wait_ge(picked_ready, 1)
            link(dve.scalar_tensor_tensor(place, PS[:, 2, 0:16], 1.0, M, ALU.add, ALU.mult))

            def by_item(a):
                return a[:, 0:16].rearrange("p (e t) -> p t e", t=2)

            dve.tensor_scalar(by_item(posx), v2(place), -1.0, None, ALU.add)
            dve.tensor_copy(by_item(gx), v2(gates))
            dve.memset(posx[:, 22:24], -1.0)
            later, over, upto, pick, prod = r[2], r[9][:, 0:8], r[9][:, 8:16], r[10][:, 0:8], r[11]
            link(dve.tensor_scalar(later, place, -1.0 - SLOT, None, ALU.add))
            link(dve.tensor_scalar(over, PS[:, 2, 16:24], float(SLOT), None, ALU.is_gt))
            link(dve.tensor_tensor_scan(upto, ones[:, 0:8], over, 0.0, ALU.mult, ALU.add))
            link(dve.tensor_scalar(items[:, 0:1], upto[:, 7:8], float(EXPERTS), None, ALU.add))
            for n in range(EXTRA):
                both = pick.unsqueeze(1).broadcast_to([P, 2, EXPERTS])
                at = 16 + 2 * n
                link(dve.scalar_tensor_tensor(pick, upto, float(n + 1), over, ALU.is_equal, ALU.mult))
                link(tt(v2(prod), v2(later), both, ALU.mult))
                link(dve.tensor_reduce(posx[:, at:at + 2], v2(prod), AX.X, ALU.add))
                link(tt(v2(prod), v2(gates), both, ALU.mult))
                link(dve.tensor_reduce(gx[:, at:at + 2], v2(prod), AX.X, ALU.add))
                link(tt(prod[:, 0:8], pick, rev[:, 0:8], ALU.mult))
                link(dve.tensor_reduce(r2[1][:, 0:1], prod[:, 0:8], AX.X, ALU.add))
                link(dve.tensor_scalar(r2[1][:, 0:1], r2[1][:, 0:1], -1.0, float(EXPERTS), ALU.mult, ALU.add))
                s = dve.tensor_scalar(items[:, n + 1:n + 2], r2[1][:, 0:1], float(EXPERTS - 1), None, ALU.min)
                if n + 1 < EXTRA:
                    link(s)
            s.then_inc(items_ready, 1)
            for t_ in range(2):
                s = dve.tensor_scalar(sel[:, t_ * SLOT:(t_ + 1) * SLOT], iota, posx[:, t_:t_ + 1], None, ALU.is_equal)
            s.then_inc(e_sel, 1)

            dve.wait_ge(items_ready, 1)
            count = dve.value_load(items[0:1, 0:1], min_val=EXPERTS, max_val=EXPERTS + EXTRA)
            with dve.Fori(0, count) as it:
                def col(a, at):
                    return a[:, bass.ds(at, 1)]

                for t_ in range(2):
                    s = dve.tensor_scalar(selg[:, t_ * SLOT:(t_ + 1) * SLOT], iota, col(posx, it * 2 + t_),
                                          col(gx, it * 2 + t_), ALU.is_equal, ALU.mult)
                s.then_inc(e_selg, 1)
                dve.wait_ge(e_gather, it + 1)
                for t_ in range(2):
                    s = dve.tensor_scalar(sel[:, t_ * SLOT:(t_ + 1) * SLOT], iota, col(posx, it * 2 + (t_ + 2)),
                                          None, ALU.is_equal)
                s.then_inc(e_sel, 1)
                for f in range(EX_UNITS):
                    dve.wait_ge(piece_done, it * PER_ITEM + (PRE + EXI["up", f] + 1))
                    dve.wait_ge(e_act, it * EX_UNITS + (f + 1))
                    if f >= 2:
                        dve.wait_ge(piece_done, it * PER_ITEM + (PRE + EXI["down", f - 2] + 1))
                    tt(e_hid_b[:, (f % 2) * 256:(f % 2 + 1) * 256], e_act_b, PS[:, 1, 0:256], ALU.mult).then_inc(e_hid, 1)
                    if f == 1:
                        dve.wait_ge(e_gtp, it + 1)
                        dve.tensor_copy(gt, PS[:, 2, 0:256]).then_inc(e_gt, 1)
                for m in range(4):
                    dve.wait_ge(e_scat, it * 4 + (m + 1))
                    for j in range(2):
                        s = residual(3, 2 * m + j, PS[:, (2, 3, 6, 7)[m], j * T:(j + 1) * T])
                    s.then_inc(e_x, 1)

            normalise(4)
            for c in range(NC):
                dve.tensor_scalar(H[:, c, :], A[:, c, :], gain(4)[:, c:c + 1], None, ALU.mult).then_inc(final_ready, 1)

        @block.gpsimd
        def _(pool):
            steps = [0]

            def link(ins):
                steps[0] += 1
                ins.then_inc(pool_step, 1)
                pool.wait_ge(pool_step, steps[0])

            def tt(o_, a, b, op):
                return pool.tensor_tensor(o_, a, b, op)

            pool.memset(ub[:, :, 0:2], 0.0).then_inc(u_padded, 1)
            pool.wait_ge(powers_ready, 1)
            pool.memset(rp_re[:, :, 7:8], 1.0)
            pool.memset(rp_im[:, :, 7:8], 0.0)
            for b in range(7):
                pool.tensor_copy(rp_re[:, :, b], fp_re[:, :, 6 - b])
                s = pool.tensor_copy(rp_im[:, :, b], fp_im[:, :, 6 - b])
            s.then_inc(reversed_ready, 1)

            pool.wait_ge(h_ready, 2 * NC)
            link(pool.memset(cz, 0.0))
            c4 = cz.rearrange("p (r t g c) -> p r t g c", r=2, t=BT, g=2)
            out4 = ct_out.rearrange("p (t r b c) -> p r t b c", t=BT, r=2, b=LB)
            tmp = buf_b[:, 1024:2048].rearrange("p (t b c) -> p t b c", t=BT, b=LB)
            for q in range(BATCHES):
                ts = slice(BT * q, BT * (q + 1))
                if q:
                    pool.wait_ge(param_psum, 9 * (q - 1) + 5)
                for g in range(2):
                    rows = slice(64 * g, 64 * g + 64)
                    link(pool.tensor_copy(c4[rows, 0, :, g, :], c_re[rows, ts, :]))
                    s = pool.tensor_scalar(c4[rows, 1, :, g, :], c_im[rows, ts, :], -1.0, None, ALU.mult)
                    if g == 0:
                        link(s)
                s.then_inc(cz_ready, 1)
                pool.wait_ge(cz_ready, q + 1)
                if q:
                    pool.wait_ge(ct_spilled, 16 * q)
                pr, pi = [a[:, ts, :].unsqueeze(3).broadcast_to([P, BT, LB, GCH]) for a in (fp_re, fp_im)]
                cr, ci = [a[:, ts, :].unsqueeze(2).broadcast_to([P, BT, LB, GCH]) for a in (c_re, c_im)]
                tt(out4[:, 0], cr, pr, ALU.mult)
                link(tt(tmp, ci, pi, ALU.mult))
                link(tt(out4[:, 0], out4[:, 0], tmp, ALU.subtract))
                tt(out4[:, 1], cr, pi, ALU.mult)
                link(tt(tmp, ci, pr, ALU.mult))
                link(tt(out4[:, 1], out4[:, 1], tmp, ALU.add))
                pool.tensor_scalar(out4[:, 1], out4[:, 1], -1.0, None, ALU.mult).then_inc(ct_ready, 1)

            pool.wait_ge(h_ready, 3 * NC)
            pool.wait_ge(t_spilled, 16 * BATCHES)
            pool.memset(xz, 0.0).then_inc(xz_zeroed, 1)
            flat_re, flat_im = phasor[:, 0:1024], phasor[:, 1024:2048]
            vr, vi, zi = vbuf[:, 0:1024], vbuf[:, 1024:2048], zbuf[:, 1024:2048]
            xr, tb = buf_a[:, 1024:2048], bb[:, 0:1024]
            pool.wait_ge(v_ready, 2)
            tt(zi, vi, flat_re, ALU.mult)
            link(tt(tb, vr, flat_im, ALU.mult))
            tt(zi, zi, tb, ALU.subtract).then_inc(z_im_ready, 1)
            pool.wait_ge(scan_ready, 1)
            tt(zi, xr, flat_im, ALU.mult)
            link(tt(tb, vr, flat_re, ALU.mult))
            pool.wait_ge(xz_zeroed, 1)
            x4 = xz.rearrange("p (r t g k) -> p r t g k", r=2, t=TILES, g=2)
            for g in range(2):
                rows = slice(64 * g, 64 * g + 64)
                tt(x4[rows, 1, :, g, 1:KB], zi.rearrange("p (t k) -> p t k", k=KB)[rows, :, 0:KB - 1],
                   tb.rearrange("p (t k) -> p t k", k=KB)[rows, :, 0:KB - 1], ALU.add).then_inc(xs_im, 1)
                pool.wait_ge(xs_im, g + 1)


def shape_constants():
    t = np.zeros((P, C_ALL), np.float32)
    t[:, C_ID:C_ID + P] = np.eye(P)
    rope = HEAD // 4
    for m in range(P):
        d = m % HEAD
        if d < rope // 2:
            t[m + rope // 2, C_ROT + m] = -1.0
        elif d < rope:
            t[m - rope // 2, C_ROT + m] = 1.0
        if d < rope:
            t[m, C_INV] = np.float32(500000.0) ** np.float32(-2.0 * (d % (rope // 2)) / rope)
    t[:, C_ONE:C_ONE + P] = 1.0
    t[:, C_TRI:C_TRI + P] = np.triu(np.ones((P, P)), 1)
    dist = np.arange(T)[:, None] - np.arange(T)[None, :]
    many = sum(((dist >= 0) & (dist <= w) & (dist % dil == 0)).astype(int) for w, dil in ((128, 1), (512, 4), (2048, 16)))
    bias = np.where(many > 0, 8.0 * np.log(np.maximum(many, 1)), -1e30)
    t[:, C_BIAS:C_BIAS + 128] = bias[:128, :128]
    t[:, C_BIAS + 128:C_BIAS + 384] = bias[128:, :]
    t[:, C_IOTA:C_IOTA + P] = np.arange(P)
    t[:, C_REV:C_REV + 16] = np.tile(8 - np.arange(8), 2)
    t[:, C_EPS] = EPS
    t[::32, C_QUAD] = 1.0
    return t


def kernel(x, c, positions, mod_w, mod_b, norm_mix_g, norm_ffn_g, ev_w_in, ev_conv_w, ev_w_out, ffn_w_gate, ffn_w_up,
           ffn_w_down, ssm_a_re, ssm_a_im, ssm_log_step, ssm_b_re, ssm_b_im, ssm_c_re, ssm_c_im, ssm_d, glu_w, glu_b,
           moe_router_w, moe_router_b, moe_w_gate, moe_w_up, moe_w_down, final_norm_g):
    import concourse.bacc as bacc
    from concourse.bass_utils import run_bass_kernel_spmd

    def columns(a):
        return np.asarray(a).reshape(-1, P).T

    def rows_in(w):
        w = np.asarray(w)
        return w.reshape(NC, P, w.shape[1] // FB, FB).transpose(2, 1, 0, 3).reshape(-1, P, PIECE)

    def rows_down(w):
        w = np.asarray(w)
        return w.reshape(w.shape[0] // FB, 2, P, D).transpose(0, 2, 1, 3).reshape(-1, P, PIECE)

    def states(a):
        a = np.asarray(a)
        a = a.reshape((TILES, P) + a.shape[2:])
        return np.moveaxis(a, 0, 1).reshape(P, -1)

    def units(gate, up, down):
        by = {"gate": rows_in(gate), "up": rows_in(up), "down": rows_down(down)}
        return [by[k][f:f + 1] for k, f in unit_order(len(by["gate"]))]

    mods = [rows_in(np.asarray(mod_w)[l]) for l in range(2)]
    w_in = rows_in(np.asarray(ev_w_in)[0])[[0, 1, 2, 3, 4, 5, 8, 9, 10, 11, 6, 7]]
    glu = rows_in(np.asarray(glu_w)[0])[[0, 4, 1, 5, 2, 6, 3, 7]]
    dense_stream = np.concatenate([mods[0][:MOD_A], w_in, mods[0][MOD_A:], rows_in(np.asarray(ev_w_out)[0]), mods[1]]
                                  + units(np.asarray(ffn_w_gate)[0], np.asarray(ffn_w_up)[0], np.asarray(ffn_w_down)[0])
                                  + [glu])
    expert_stream = np.concatenate([p for e in range(EXPERTS) for p in units(
        np.asarray(moe_w_gate)[0, e], np.asarray(moe_w_up)[0, e], np.asarray(moe_w_down)[0, e])])
    mix_g, ffn_g = np.asarray(norm_mix_g), np.asarray(norm_ffn_g)
    small = np.concatenate([
        columns(c), columns(mod_b), columns(mix_g[0]), columns(ffn_g[0]), columns(mix_g[1]), columns(ffn_g[1]),
        columns(final_norm_g), columns(np.asarray(ev_conv_w)[0]), columns(ssm_d), columns(glu_b),
        states(np.asarray(ssm_a_re)[0]), states(np.asarray(ssm_a_im)[0]),
        states(np.repeat(np.asarray(ssm_log_step)[0][:, None], STATES, 1)),
        np.broadcast_to(np.tile(np.asarray(moe_router_b)[0], 2), (P, 16)),
        np.asarray(moe_router_w)[0].reshape(NC, P, EXPERTS).transpose(1, 0, 2).reshape(P, -1)], axis=1)
    ssm_small = np.concatenate([states(np.asarray(ssm_b_re)[0]), states(np.asarray(ssm_b_im)[0]),
                                states(np.asarray(ssm_c_re)[0].transpose(0, 2, 1)),
                                states(np.asarray(ssm_c_im)[0].transpose(0, 2, 1))], axis=1)
    arrays = {
        "xt": np.asarray(x)[0].T.reshape(NC, P, T).transpose(1, 0, 2).reshape(P, -1),
        "positions": np.asarray(positions), "small": small, "consts": shape_constants(), "ssm_small": ssm_small,
        "dense_stream": dense_stream, "expert_stream": expert_stream,
    }
    arrays = {"in_" + n: np.ascontiguousarray(a) for n, a in arrays.items()}
    nc = bacc.Bacc("TRN2", target_bir_lowering=False, num_devices=1)
    args = [nc.dram_tensor(n, a.shape, mybir.dt.from_np(a.dtype), kind="ExternalInput").ap() for n, a in arrays.items()]
    h_scr = nc.dram_tensor("h_scratch", (D, T), F32, kind="Internal").ap()
    y_scr = nc.dram_tensor("y_scratch", (D, T), F32, kind="Internal").ap()
    ssm_scr = nc.dram_tensor("ssm_scratch", (SSM, P, PIECE), F32, kind="Internal").ap()
    out = nc.dram_tensor("out_t", (P, NC * T), F32, kind="ExternalOutput").ap()
    trunk_kernel(nc, *args, h_scr, y_scr, ssm_scr, out)
    res = run_bass_kernel_spmd(nc, [arrays], core_ids=[0]).results[0]["out_t"]
    return np.asarray(res).reshape(P, NC, LB, KB).transpose(3, 2, 1, 0).reshape(1, T, D)
```

```python
from contextlib import ExitStack

import numpy as np

import concourse.bass as bass
from concourse import mybir

ALU = mybir.AluOpType
ACT = mybir.ActivationFunctionType
AX = mybir.AxisListType
F32 = mybir.dt.float32
I32 = mybir.dt.int32

P = 128
D = 1024
T = 256
NC = D // P
EPS = 1e-6
HEADS, HEAD = 8, 64
D_FF = 2816
D_FFE = 3584
EXPERTS = 8
FB = 256
FF_UNITS = D_FF // FB
EX_UNITS = D_FFE // FB
SLOT = 128
HALF = SLOT // 2
EXTRA = (2 * T) // (SLOT + 1)
assert T <= 2 * SLOT

GROUPS, GCH, STATES = 64, 16, 64
LB = P // GCH
KB = T // LB
TILES = GROUPS * STATES // P
BATCHES = 4
BT = TILES // BATCHES

RING = 14
PIECE = 2048
W_IN, W_OUT, SSM, GLU = 12, 4, 3 * BATCHES, 8
MOD_GROUPS = 24
DENSE = 2 * MOD_GROUPS + W_IN + W_OUT + 3 * FF_UNITS
PRE = DENSE + SSM + GLU
PER_ITEM = 3 * EX_UNITS
assert PER_ITEM % RING == 0

C_ID, C_ROT, C_ONE, C_TRI, C_BIAS, C_IOTA, C_REV, C_INV = 0, 240, 368, 496, 624, 1008, 1136, 1152
C_EPS, C_QUAD = 1153, 1154
C_ALL = 1155
K_C, K_MODB, K_GAIN, K_CONV, K_D, K_GLUB, K_ARE, K_AIM, K_LS, K_RB, K_RW = 0, 8, 104, 144, 156, 164, 180, 212, 244, 276, 292
K_ALL = 356

MAGIC = 12582912.0
PI_LOW = 3.1415925


def two_pi_parts():
    full = 2 * np.pi
    first = 6.28125
    second = float(np.float32(np.round((full - first) * 2 ** 20) / 2 ** 20))
    return first, second, float(np.float32(full - first - second))


def unit_order(units):
    order = []
    for f in range(units):
        order += [("gate", f), ("up", f)]
        if f:
            order.append(("down", f - 1))
    return order + [("down", units - 1)]


def unit_index(units):
    return {key: n for n, key in enumerate(unit_order(units))}


def side_plan():
    uses = {("param", 0): 2, ("param", 1): 2, ("param", 2): 1, ("param", 3): 2, ("param", 4): 2}
    at = {}
    for q in range(BATCHES):
        for s in range(5):
            at.setdefault(5 + 7 * q + s, []).append(("param", q, s))
    segments = [n for n in range(3 * FF_UNITS + 1) if n != 2]
    free = [n for n in segments if n not in at and n < 3 * FF_UNITS]
    for g, n in zip(range(MOD_GROUPS // 2, MOD_GROUPS), free):
        at.setdefault(n, []).append(("rows", g, 0))
        at.setdefault(segments[segments.index(n) + 1], []).insert(0, ("turn", g, 0))
    plan, use = {}, 0
    for n in segments:
        for kind, i, s in at.get(n, []):
            plan.setdefault(n, []).append((kind, i, s, use))
            use += uses.get((kind, s), 1)
    return plan


PLAN = side_plan()
USE = {(kind, i, s): use for steps in PLAN.values() for kind, i, s, use in steps}
ROW_USES = [use for (kind, _, _), use in USE.items() if kind == "rows"]


def psum_count(use):
    return use + 1 - sum(u < use for u in ROW_USES)



def stream_order():
    def mod(a, b):
        return [("mod", i) for i in range(2 * a, 2 * b)]

    order = mod(0, 4) + [("in", w) for w in range(W_IN)] + mod(4, 10) + [("out", w) for w in range(W_OUT)] + mod(10, 12)

    def side(n):
        return [p for kind, g, _, _ in PLAN.get(n, []) if kind == "rows" for p in mod(g, g + 1)]

    for f in range(FF_UNITS):
        order += [("gate", f)] + side(3 * f) + [("up", f)] + side(3 * f + 1)
        if f:
            order += [("down", f - 1)] + side(3 * f + 2)
    return order + [("down", FF_UNITS - 1)]


ORDER = stream_order()
AT = {key: n for n, key in enumerate(ORDER)}
assert len(ORDER) == DENSE


def trunk_kernel(nc, xt_in, pos_in, cols_in, consts_in, ssm_in, dense_in, expert_in, h_scr, y_scr, ssm_scr, out):
    ctx = ExitStack()
    with ctx:
        def sb(name, cols, dt=F32):
            return ctx.enter_context(nc.sbuf_tensor(name, [P, cols], dt))

        def sem(name):
            return ctx.enter_context(nc.semaphore(name))

        PS = ctx.enter_context(nc.psum_tensor("PS", [P, 8, 512], F32))
        ring = sb("ring", RING * PIECE)
        buf_a = sb("buf_a", NC * T)
        buf_b = sb("buf_b", NC * T)
        buf_h = sb("buf_h", NC * T)
        consts = sb("consts", C_ALL)
        cols = sb("cols", K_ALL)
        ssm_par = sb("ssm_par", 4 * TILES * GCH)
        bb = sb("bb", 2 * TILES * GCH)
        pows = sb("pows", 4 * TILES * LB)
        phasor = sb("phasor", 2 * TILES * KB)
        work = sb("work", 10240)
        modc = sb("modc", 96)
        acol = sb("acol", 4 * NC)
        stat = sb("stat", T)
        items = sb("items", 1 + EXTRA + EXPERTS + EXTRA, I32)
        m8 = sb("m8", TILES)

        def chunked(b):
            return b[:, :].rearrange("p (c t) -> p c t", c=NC)

        A, B, H = chunked(buf_a), chunked(buf_b), chunked(buf_h)

        def resid(k):
            return A if k < 2 else B

        def scratch(k):
            return B if k < 2 else A

        ident = consts[:, C_ID:C_ID + P]
        rot = consts[:, C_ROT:C_ROT + P]
        ones = consts[:, C_ONE:C_ONE + P]
        tri = consts[:, C_TRI:C_TRI + P]
        att_bias = consts[:, C_BIAS:C_BIAS + 384]
        iota = consts[:, C_IOTA:C_IOTA + P]
        rev = consts[:, C_REV:C_REV + 16]

        o = 0

        def take(n):
            nonlocal o
            o += n
            assert o <= 10240
            return work[:, o - n:o]

        qT, kT, vT, bg = take(1024), take(1024), take(1024), take(1024)
        ub = take(4 * (T + 2)).rearrange("p (c t) -> p c t", c=4)
        sco, ptb = take(768), take(768)
        cosF, rtmp = take(288), take(512)
        sinF = take(288)
        ang, ang_k, sin_h = take(288), take(288), take(288)
        att_st = take(64)
        cond32 = take(NC * 32)
        mod_row = take(512)
        posi = take(T).bitcast(I32)
        s_cols = [take(TILES) for _ in range(15)]
        o = 0
        bsm, bt_out, ct_out, t_out = take(2048), take(2048), take(2048), take(2048)
        f_act, f_hid = take(512), take(1024)
        cz, kc = take(512), stat[:, :]
        o = 0
        ust, vbuf, zbuf, xz = take(2048), take(2048), take(2048), take(4096)
        y_sb = vbuf
        gT = zbuf.rearrange("p (c t) -> p c t", c=NC)
        sig = ust
        o = 0
        h_tm, hgT = take(2048), take(1024)
        e_act_b, e_hid_b, sel, selg, gt, ye = take(256), take(512), take(256), take(256), take(256), take(1024)
        posx, gx = take(24), take(24)
        r = [take(16) for _ in range(12)]
        r2 = [take(2) for _ in range(8)]
        few, fold, iota_item = take(EXPERTS + EXTRA), take(SLOT), take(SLOT)

        mod_bT = cols[:, K_MODB:K_MODB + 96]

        def gain(k):
            return cols[:, K_GAIN + 8 * k:K_GAIN + 8 * k + 8]

        def part(k, which):
            at = 48 * (k // 2) + 24 * (k % 2) + 8 * which
            return modc[:, at:at + 8]

        ssm = [ssm_par[:, i * 512:(i + 1) * 512].rearrange("p (t c) -> p t c", c=GCH) for i in range(4)]
        b_re, b_im, c_re, c_im = ssm
        cond_late, row_late = ssm_par[:, 0:NC * 32], ssm_par[:, 512:1024]
        bb_re, bb_im = [bb[:, i * 512:(i + 1) * 512].rearrange("p (t c) -> p t c", c=GCH) for i in range(2)]
        rp_re, rp_im, fp_re, fp_im = [pows[:, i * 256:(i + 1) * 256].rearrange("p (t b) -> p t b", b=LB)
                                      for i in range(4)]
        ph_re, ph_im = [phasor[:, i * 1024:(i + 1) * 1024].rearrange("p (t k) -> p t k", k=KB) for i in range(2)]

        ring_full = [sem(f"ring_full{s}") for s in range(RING)]
        row_evac, mod_cols, cond_moved = sem("row_evac"), sem("mod_cols"), sem("cond_moved")
        piece_done = sem("piece_done")
        (cols_loaded, x_loaded, tables_loaded, ssm_loaded, dve_step,) = [sem(n) for n in "cols_loaded x_loaded tables_loaded ssm_loaded dve_step".split()]
        (act_step, pool_step, cond_exp, cond_ready, dt_ready,) = [sem(n) for n in "act_step pool_step cond_exp cond_ready dt_ready".split()]
        (decay_arg, mag_ready, angle_ready, sines_ready, powers_ready,) = [sem(n) for n in "decay_arg mag_ready angle_ready sines_ready powers_ready".split()]
        (reversed_ready, squares_ready, sumsq_ready, rms_ready, h_ready,) = [sem(n) for n in "reversed_ready squares_ready sumsq_ready rms_ready h_ready".split()]
        (x_updated, mod_taken, proj_act, proj_dve, rope_psum,) = [sem(n) for n in "x_updated mod_taken proj_act proj_dve rope_psum".split()]
        (rope_ready, u_padded, scores_ready, masked_ready, negmax_ready,) = [sem(n) for n in "rope_ready u_padded scores_ready masked_ready negmax_ready".split()]
        (exp_ready, probs_ready, pt_psum, pt_ready, pv_ready,) = [sem(n) for n in "exp_ready probs_ready pt_psum pt_ready pv_ready".split()]
        (attn_out, conv_out, gate_act, hid_ready, bsm_ready,) = [sem(n) for n in "attn_out conv_out gate_act hid_ready bsm_ready".split()]
        (ct_ready, cz_ready, param_psum, param_evac, bt_spilled,) = [sem(n) for n in "ct_ready cz_ready param_psum param_evac bt_spilled".split()]
        (ct_spilled, t_spilled, h_stored, u_loaded, v_ready,) = [sem(n) for n in "ct_spilled t_spilled h_stored u_loaded v_ready".split()]
        (z_im_ready, scan_ready, xs_re, xs_im, y_evac, xz_zeroed, y_sum) = [sem(n) for n in "z_im_ready scan_ready xs_re xs_im y_evac xz_zeroed y_sum".split()]
        (y_stored, y_loaded, yd_ready, gelu_ready, sig_ready,) = [sem(n) for n in "y_stored y_loaded yd_ready gelu_ready sig_ready".split()]
        (logits_ready, htm_psum, htm_ready, picked_ready, gap_ready,) = [sem(n) for n in "logits_ready htm_psum htm_ready picked_ready gap_ready".split()]
        (pick_exp, pos_ready, items_ready, e_act, e_hid,) = [sem(n) for n in "pick_exp pos_ready items_ready e_act e_hid".split()]
        (e_sel, e_selg, e_gtp, e_gt, e_gather,) = [sem(n) for n in "e_sel e_selg e_gtp e_gt e_gather".split()]
        (e_iota, e_hg, e_y, e_scat, e_x, final_ready,) = [sem(n) for n in "e_iota e_hg e_y e_scat e_x final_ready".split()]
        (out_stored,) = [sem(n) for n in "out_stored".split()]

        def slot(n):
            return ring[:, (n % RING) * PIECE:(n % RING + 1) * PIECE]

        block = ctx.enter_context(nc.Block())

        @block.sync
        def _(sp):
            def load(n, src):
                if n >= RING:
                    sp.wait_ge(piece_done, n - RING + 1)
                sp.dma_start(slot(n), src).then_inc(ring_full[n % RING], 16)

            for n in range(DENSE):
                load(n, dense_in[n])
            sp.wait_ge(bt_spilled, 16 * BATCHES)
            sp.wait_ge(ct_spilled, 16 * BATCHES)
            sp.wait_ge(t_spilled, 16 * BATCHES)
            for n in range(SSM):
                load(DENSE + n, ssm_scr[n])
            for n in range(GLU):
                load(DENSE + SSM + n, dense_in[DENSE + n])

            def expert(e, item):
                for j in range(PER_ITEM):
                    n = PRE + j
                    sp.wait_ge(piece_done, item * PER_ITEM + (n - RING + 1))
                    sp.dma_start(slot(n), expert_in[bass.ds(e * PER_ITEM + j, 1)].rearrange("o p n -> (o p) n")).then_inc(
                        ring_full[n % RING], 16)

            with sp.Fori(0, EXPERTS) as e:
                expert(e, e)
            sp.wait_ge(items_ready, 1)
            count = sp.value_load(items[0:1, 0:1], min_val=EXPERTS, max_val=EXPERTS + EXTRA)
            for extra in range(EXTRA):
                with sp.If(count > EXPERTS + extra):
                    e = sp.value_load(items[0:1, 1 + extra:2 + extra], min_val=0, max_val=EXPERTS - 1)
                    expert(e, EXPERTS + extra)

        EXI = unit_index(EX_UNITS)
        AT_BT, AT_T, AT_CT = DENSE, DENSE + BATCHES, DENSE + 2 * BATCHES
        AT_GLU = DENSE + SSM

        @block.tensor
        def _(pe):
            used = [0]

            def piece():
                n = used[0]
                pe.wait_ge(ring_full[n % RING], 16 * (n // RING + 1))
                used[0] += 1
                return slot(n)

            def k_chunks(w):
                return w.rearrange("p (c n) -> p c n", c=NC)

            def sums(k, bank):
                for cp in range(4):
                    pe.wait_ge(squares_ready, 4 * k + cp + 1)
                    for c in (2 * cp, 2 * cp + 1):
                        mm = pe.matmul(PS[:, bank, 0:T], ones, scratch(k)[:, c, :], start=(c == 0), stop=(c == NC - 1))
                mm.then_inc(sumsq_ready, 1)

            def mod_rows(g, bank=6, cond=cond32):
                for j in range(2):
                    w = k_chunks(piece())
                    for c in range(NC):
                        q = 32 * (c % 4)
                        mm = pe.matmul(PS[q:q + 32, bank, j * FB:(j + 1) * FB], cond[:, 32 * c:32 * c + 32], w[:, c, :],
                                       start=(c < 4), stop=(c >= 4))
                    mm.then_inc(piece_done, 1)

            def turned_rows(bank, at, rows):
                for m in range(4):
                    mm = pe.matmul(PS[:, bank, at + m:at + m + 1], rows[:, m * P:(m + 1) * P],
                                   consts[:, C_QUAD:C_QUAD + 1], start=True, stop=True)
                return mm

            def mod_turn(g):
                pe.wait_ge(row_evac, g + 1)
                turned_rows(7, 4 * g, mod_row).then_inc(mod_cols, 1)

            def dense(bank, moving, chunk_sem=None, chunk_base=0):
                w = k_chunks(piece())
                for j in range(2):
                    for c in range(NC):
                        if chunk_sem is not None and j == 0:
                            pe.wait_ge(chunk_sem, chunk_base + c + 1)
                        mm = pe.matmul(PS[:, bank, j * T:(j + 1) * T], w[:, c, j * P:(j + 1) * P], moving[:, c, :],
                                       start=(c == 0), stop=(c == NC - 1))
                mm.then_inc(piece_done, 1)

            pe.wait_ge(tables_loaded, 32)
            pe.wait_ge(cond_ready, 1)
            for g in range(4):
                if g == 2:
                    sums(0, 0)
                mod_rows(g)
                mod_turn(g)

            def rope(s):
                pe.wait_ge(proj_act, s + 1)
                if s >= 2:
                    pe.wait_ge(rope_ready, s - 1)
                src = (qT, kT)[s // 2]
                pe.matmul(PS[:, 3 + s % 2, :], rot, src[:, (s % 2) * 512:(s % 2 + 1) * 512], start=True,
                          stop=True).then_inc(rope_psum, 1)

            for w in range(W_IN):
                if w >= 2:
                    if w - 2 in (8, 9):
                        pe.wait_ge(proj_dve, w - 9)
                    else:
                        pe.wait_ge(proj_act, w - 1)
                bank = 1 + w % 2
                if w in (4, 5):
                    wv = k_chunks(piece())
                    for tt in range(2):
                        for c in range(NC):
                            mm = pe.matmul(PS[:, bank, tt * T:(tt + 1) * T], H[:, c, tt * P:(tt + 1) * P], wv[:, c, :],
                                           start=(c == 0), stop=(c == NC - 1))
                    mm.then_inc(piece_done, 1)
                elif w == 0:
                    dense(bank, H, h_ready, 0)
                else:
                    dense(bank, H)
                if 4 <= w <= 7:
                    rope(w - 4)

            def score(h):
                pe.wait_ge(rope_ready, 4)
                if h >= 2:
                    pe.wait_ge(masked_ready, h - 1)
                r0, ch, bank = HEAD * (h % 2), (h // 2) * T, 3 + h % 2
                pe.matmul(PS[:, bank, 0:128], qT[r0:r0 + 64, ch:ch + 128], kT[r0:r0 + 64, ch:ch + 128],
                          start=True, stop=True)
                pe.matmul(PS[:, bank, 128:384], qT[r0:r0 + 64, ch + 128:ch + 256], kT[r0:r0 + 64, ch:ch + 256],
                          start=True, stop=True).then_inc(scores_ready, 1)

            def turn(h):
                pe.wait_ge(probs_ready, h + 1)
                if h >= 2:
                    pe.wait_ge(pt_ready, h - 1)
                s = sco[:, (h % 2) * 384:(h % 2 + 1) * 384]
                for i in range(3):
                    mm = pe.transpose(PS[:, (5, 0)[h % 2], i * P:(i + 1) * P], s[:, i * P:(i + 1) * P], ident)
                mm.then_inc(pt_psum, 1)

            def attend(h):
                pe.wait_ge(pt_ready, h + 1)
                if h // 2 >= 2:
                    pe.wait_ge(attn_out, h // 2 - 1)
                pt = ptb[:, (h % 2) * 384:(h % 2 + 1) * 384]
                r0, bank = HEAD * (h % 2), 1 + (h // 2) % 2
                pe.matmul(PS[r0:r0 + 64, bank, 0:256], vT[:, h * 64:(h + 1) * 64], pt[:, 0:256], start=True, stop=False,
                          skip_group_check=True)
                pe.matmul(PS[r0:r0 + 64, bank, 128:256], vT[:, 512 + h * 64:512 + (h + 1) * 64], pt[:, 256:384],
                          start=False, stop=True, skip_group_check=True).then_inc(pv_ready, 1)

            pe.wait_ge(proj_act, 10)
            pe.wait_ge(proj_dve, 2)
            score(0)
            score(1)
            for h in range(HEADS):
                if 1 <= h <= 6:
                    mod_turn(3 + h)
                if h < 6:
                    mod_rows(4 + h)
                turn(h)
                if h + 2 < HEADS:
                    score(h + 2)
                if h:
                    attend(h - 1)
            attend(HEADS - 1)

            pe.wait_ge(attn_out, 4)
            pe.wait_ge(conv_out, 4)
            for w in range(W_OUT):
                if w >= 2:
                    pe.wait_ge(x_updated, 2 * (w - 1))
                dense(3 + w % 2, H)

            sums(1, 2)
            for g in (10, 11):
                mod_rows(g)
                mod_turn(g)

            def side_bank(u):
                if u >= 2:
                    pe.wait_ge(param_evac, u - 1)
                return 2 + u % 2

            def param_step(q, s, use):
                if s in (0, 1):
                    if s == 0:
                        pe.wait_ge(bsm_ready, q + 1)
                    for half in range(2):
                        bank = side_bank(use + half)
                        for i in range(4):
                            tile, ri = 4 * s + 2 * half + i // 2, i % 2
                            mm = pe.transpose(PS[:, bank, i * P:(i + 1) * P],
                                              bsm[:, ri * 1024 + tile * P:ri * 1024 + (tile + 1) * P], ident)
                        mm.then_inc(param_psum, 1)
                if s == 2:
                    pe.wait_ge(cz_ready, q + 1)
                    bank = side_bank(use)
                    for tile in range(BT):
                        for ri in range(2):
                            mm = pe.matmul(PS[:, bank, tile * 32:(tile + 1) * 32],
                                           bsm[:, ri * 1024 + tile * P:ri * 1024 + (tile + 1) * P],
                                           cz[:, ri * 256 + tile * 32:ri * 256 + (tile + 1) * 32],
                                           start=(ri == 0), stop=(ri == 1))
                    mm.then_inc(param_psum, 1)
                if s in (3, 4):
                    pe.wait_ge(param_evac, USE["param", q, 2] + 1)
                    for half in range(2):
                        bank = side_bank(use + half)
                        for i in range(2):
                            b = 4 * (s - 3) + 2 * half + i
                            off = C_ID + GCH * (LB - 1 - b)
                            mm = pe.matmul(PS[:, bank, i * 256:(i + 1) * 256], consts[:, off:off + P], kc,
                                           start=True, stop=True)
                        mm.then_inc(param_psum, 1)

            def segment(n):
                for kind, i, s, use in PLAN.get(n, []):
                    if kind == "param":
                        param_step(i, s, use)
                    elif kind == "rows":
                        mod_rows(i, side_bank(use), cond_late)
                    else:
                        pe.wait_ge(param_evac, USE["rows", i, 0] + 1)
                        turned_rows(side_bank(use), 0, row_late).then_inc(param_psum, 1)

            def down(f):
                pe.wait_ge(hid_ready, f + 1)
                if f == 0:
                    pe.wait_ge(mod_taken, 3)
                w = piece()
                for j in range(2):
                    for n in range(NC):
                        mm = pe.matmul(PS[:, 4 + n // 2, (n % 2) * T:(n % 2 + 1) * T],
                                       w[:, j * D + n * P:j * D + (n + 1) * P],
                                       f_hid[:, (f % 2) * 512 + j * T:(f % 2) * 512 + (j + 1) * T],
                                       start=(f == 0 and j == 0 and n % 2 == 0), stop=(f == FF_UNITS - 1 and j == 1),
                                       skip_group_check=True)
                mm.then_inc(piece_done, 1)

            for f in range(FF_UNITS):
                if f:
                    pe.wait_ge(gate_act, f)
                    dense(0, H)
                else:
                    dense(0, H, h_ready, NC)
                    pe.wait_ge(cond_moved, 1)
                segment(3 * f)
                if f:
                    pe.wait_ge(hid_ready, f)
                dense(1, H)
                segment(3 * f + 1)
                if f:
                    down(f - 1)
                    segment(3 * f + 2)
            down(FF_UNITS - 1)
            segment(3 * FF_UNITS)

            sums(2, 0)
            pe.wait_ge(u_loaded, 16 * LB)
            for q in range(BATCHES):
                w = piece().rearrange("p (t r m) -> p t r m", t=BT, r=2)
                for tl in range(BT):
                    at, n = (BT * q + tl) * 64, min(128, 512 - 64 * tl)
                    for ri in range(2):
                        mm = pe.matmul(PS[:, 4 * ri + q, tl * 64:tl * 64 + n], w[:, tl, ri, :], ust[:, at:at + n],
                                       start=True, stop=True)
                mm.then_inc(piece_done, 1)
            for q in range(BATCHES):
                w = piece().rearrange("p (g m) -> p g m", g=16)
                pe.wait_ge(v_ready, 4 * q + 2)
                for gl in range(16):
                    at, n = (16 * q + gl) * KB, min(128, 512 - KB * gl)
                    mm = pe.matmul(PS[:, 4 + q, gl * KB:gl * KB + n], w[:, gl, :], ust[:, at:at + n], start=True, stop=True)
                mm.then_inc(piece_done, 1)
            pe.wait_ge(xs_re, 2)
            pe.wait_ge(xs_im, 2)
            for q in range(BATCHES):
                w = piece().rearrange("p (t r m) -> p t r m", t=BT, r=2)
                for tl in range(BT):
                    at, n = (BT * q + tl) * 64, min(128, 512 - 64 * tl)
                    for ri in range(2):
                        mm = pe.matmul(PS[:, q, tl * 64:tl * 64 + n], w[:, tl, ri, :],
                                       xz[:, ri * 2048 + at:ri * 2048 + at + n], start=(ri == 0), stop=(ri == 1))
                mm.then_inc(piece_done, 1)

            for i in range(4):
                if i >= 2:
                    pe.wait_ge(x_updated, 16 + 2 * (i - 1))
                if i == 0:
                    pe.wait_ge(gelu_ready, 4)
                dense(i % 2, gT)
                dense(2 + i % 2, gT)

            sums(3, 4)
            pe.wait_ge(h_ready, 4 * NC)
            for tt in range(2):
                for c in range(NC):
                    mm = pe.matmul(PS[:, 5, tt * 8:tt * 8 + 8], H[:, c, tt * P:(tt + 1) * P],
                                   cols[:, K_RW + 8 * c:K_RW + 8 * c + 8], start=(c == 0), stop=(c == NC - 1))
            mm.then_inc(logits_ready, 1)
            for m in range(4):
                for i in range(4):
                    tt, c = (4 * m + i) // NC, (4 * m + i) % NC
                    mm = pe.transpose(PS[:, (6, 7, 0, 1)[m], i * P:(i + 1) * P], H[:, c, tt * P:(tt + 1) * P], ident)
                mm.then_inc(htm_psum, 1)
            pe.wait_ge(picked_ready, 1)
            M = r[7]
            pe.matmul(PS[:, 2, 0:8], tri, M[:, 0:8], start=True, stop=True)
            pe.matmul(PS[:, 2, 8:16], tri, M[:, 8:16], start=True, stop=False)
            pe.matmul(PS[:, 2, 8:16], ones, M[:, 0:8], start=False, stop=True)
            pe.matmul(PS[:, 2, 16:24], ones, M[:, 0:8], start=True, stop=False)
            pe.matmul(PS[:, 2, 16:24], ones, M[:, 8:16], start=False, stop=True).then_inc(pos_ready, 1)

            def gather():
                for c in range(NC):
                    for tt in range(2):
                        mm = pe.matmul(PS[:, 6 + c // 4, (c % 4) * SLOT:(c % 4 + 1) * SLOT],
                                       h_tm[:, tt * D + c * P:tt * D + (c + 1) * P], sel[:, tt * SLOT:(tt + 1) * SLOT],
                                       start=(tt == 0), stop=(tt == 1))
                mm.then_inc(e_gather, 1)

            pe.wait_ge(htm_ready, 4)
            pe.wait_ge(e_sel, 1)
            gather()
            pe.wait_ge(items_ready, 1)
            count = pe.value_load(items[0:1, 0:1], min_val=EXPERTS, max_val=EXPERTS + EXTRA)
            with pe.Fori(0, count) as it:
                def e_piece(key):
                    n = PRE + EXI[key]
                    pe.wait_ge(ring_full[n % RING], it * (16 * PER_ITEM // RING) + 16 * (n // RING + 1))
                    return slot(n)

                def into(bank, w):
                    w = k_chunks(w)
                    for j in range(2):
                        for c in range(NC):
                            mm = pe.matmul(PS[:, bank, j * SLOT:(j + 1) * SLOT], w[:, c, j * P:(j + 1) * P],
                                           hgT[:, c * SLOT:(c + 1) * SLOT], start=(c == 0), stop=(c == NC - 1))
                    mm.then_inc(piece_done, 1)

                def e_down(f, small):
                    pe.wait_ge(e_hid, it * EX_UNITS + (f + 1))
                    w = e_piece(("down", f))
                    for n in range(2):
                        for j in range(2):
                            at = (f % 2) * 256 + j * SLOT
                            if small:
                                mm = pe.matmul(PS[HALF * j:HALF * (j + 1), 4 + n, :], e_hid_b[:, at:at + HALF],
                                               w[:, j * D + n * 512:j * D + (n + 1) * 512],
                                               start=(f == 0), stop=(f == EX_UNITS - 1))
                            else:
                                mm = pe.matmul(PS[:, 4 + n, :], e_hid_b[:, at:at + SLOT],
                                               w[:, j * D + n * 512:j * D + (n + 1) * 512],
                                               start=(f == 0 and j == 0), stop=(f == EX_UNITS - 1 and j == 1))
                    mm.then_inc(piece_done, 1)

                def swiglu(small):
                    for f in range(EX_UNITS):
                        if f:
                            pe.wait_ge(e_act, it * EX_UNITS + f)
                        into(0, e_piece(("gate", f)))
                        if f:
                            pe.wait_ge(e_hid, it * EX_UNITS + f)
                        into(1, e_piece(("up", f)))
                        if f == 1:
                            pe.wait_ge(e_selg, it + 1)
                            for tt in range(2):
                                mm = pe.transpose(PS[:, 2, tt * P:(tt + 1) * P], selg[:, tt * P:(tt + 1) * P], ident)
                            mm.then_inc(e_gtp, 1)
                        if f:
                            e_down(f - 1, small)
                    pe.wait_ge(e_sel, it + 2)
                    gather()
                    e_down(EX_UNITS - 1, small)

                pe.wait_ge(e_hg, it + 1)
                small_item = pe.value_load(items[0:1, bass.ds(it + (1 + EXTRA), 1)], min_val=0, max_val=1)
                with pe.If(small_item > 0):
                    swiglu(True)
                with pe.If(small_item < 1):
                    swiglu(False)
                pe.wait_ge(e_y, it + 1)
                pe.wait_ge(e_gt, it + 1)
                pe.wait_ge(e_hg, it + 2)
                for m in range(4):
                    for j in range(2):
                        n = 2 * m + j
                        mm = pe.matmul(PS[:, (2, 3, 6, 7)[m], j * T:(j + 1) * T], ye[:, n * P:(n + 1) * P], gt,
                                       start=True, stop=True)
                    mm.then_inc(e_scat, 1)

            sums(4, 0)

        @block.scalar
        def _(act):
            steps = [0]

            def copy(out_ap, in_ap):
                return act.activation(out_ap, in_ap, ACT.Copy)

            act.dma_start(cols[:, :], cols_in).then_inc(cols_loaded, 16)
            act.dma_start(consts[:, :], consts_in).then_inc(tables_loaded, 16)
            act.dma_start(buf_a[:, :], xt_in).then_inc(x_loaded, 16)
            act.dma_start(posi, pos_in.partition_broadcast(P).rearrange("p o t -> p (o t)")).then_inc(tables_loaded, 16)
            act.dma_start(ssm_par[:, :], ssm_in).then_inc(ssm_loaded, 16)

            act.wait_ge(cols_loaded, 16)
            act.activation(att_st[:, 0:8], cols[:, K_C:K_C + 8], ACT.Exp, scale=-1.0).then_inc(cond_exp, 1)
            act.activation(s_cols[0], cols[:, K_LS:K_LS + 32], ACT.Exp).then_inc(dt_ready, 1)

            def take_rows(n, group):
                for g in range(group, group + n):
                    act.wait_ge(piece_done, AT["mod", 2 * g + 1] + 1)
                    copy(mod_row, PS[:, 6, :]).then_inc(row_evac, 1)

            def squares(k, wait):
                for cp in range(4):
                    wait(cp)
                    act.activation(scratch(k)[:, 2 * cp:2 * cp + 2, :], resid(k)[:, 2 * cp:2 * cp + 2, :],
                                   ACT.Square).then_inc(squares_ready, 1)

            def root(k, bank):
                act.wait_ge(sumsq_ready, k + 1)
                act.activation(stat[:, :], PS[:, bank, 0:T], ACT.Sqrt, scale=1.0 / D,
                               bias=consts[:, C_EPS:C_EPS + 1]).then_inc(rms_ready, 1)

            def x_wait(k):
                return lambda cp: act.wait_ge(x_updated, 8 * (k - 1) + 2 * (cp + 1))

            act.wait_ge(x_loaded, 16)
            squares(0, lambda cp: None)
            take_rows(2, 0)
            act.wait_ge(tables_loaded, 32)
            root(0, 0)
            take_rows(2, 2)
            act.wait_ge(decay_arg, 1)
            act.activation(s_cols[2], s_cols[1], ACT.Exp).then_inc(mag_ready, 1)
            act.wait_ge(angle_ready, 1)
            act.activation(sinF, ang, ACT.Sin).then_inc(sines_ready, 1)
            act.activation(sin_h, ang, ACT.Sin, scale=0.5).then_inc(sines_ready, 1)

            for w in (0, 1, 2, 3, 4, 5, 6, 7, 10, 11):
                act.wait_ge(piece_done, AT["in", w] + 1)
                src = PS[:, 1 + w % 2, :]
                if w < 4:
                    copy((qT, kT)[w // 2][:, (w % 2) * 512:(w % 2 + 1) * 512], src).then_inc(proj_act, 1)
                elif w < 6:
                    copy(vT.rearrange("p (t n) -> p t n", t=2)[:, :, (w - 4) * 256:(w - 3) * 256],
                         src.rearrange("p (t n) -> p t n", t=2)).then_inc(proj_act, 1)
                elif w < 8:
                    copy(ub[:, 2 * (w - 6):2 * (w - 6) + 2, 2:T + 2],
                         src.rearrange("p (c t) -> p c t", c=2)).then_inc(proj_act, 1)
                else:
                    copy(bg[:, (w - 10) * 512:(w - 9) * 512], src).then_inc(proj_act, 1)

            def exps(h):
                act.wait_ge(negmax_ready, h + 1)
                s = sco[:, (h % 2) * 384:(h % 2 + 1) * 384]
                nm = att_st[:, 16 + 2 * h:18 + 2 * h]
                l = att_st[:, 32 + 2 * h:34 + 2 * h]
                act.activation(s[:, 0:128], s[:, 0:128], ACT.Exp, bias=nm[:, 0:1], scale=0.125, accum_out=l[:, 0:1])
                act.activation(s[:, 128:384], s[:, 128:384], ACT.Exp, bias=nm[:, 1:2], scale=0.125,
                               accum_out=l[:, 1:2]).then_inc(exp_ready, 1)

            exps(0)
            for h in range(HEADS):
                if h + 1 < HEADS:
                    exps(h + 1)
                if h < 6:
                    take_rows(1, 4 + h)
                act.wait_ge(pt_psum, h + 1)
                if h >= 2:
                    act.wait_ge(pv_ready, h - 1)
                copy(ptb[:, (h % 2) * 384:(h % 2 + 1) * 384], PS[:, (5, 0)[h % 2], 0:384]).then_inc(pt_ready, 1)

            squares(1, x_wait(1))
            root(1, 2)
            take_rows(2, 10)

            def param_take(u, out_ap, n, view=None):
                act.wait_ge(param_psum, psum_count(u))
                src = PS[:, 2 + u % 2, 0:n]
                copy(out_ap, src if view is None else view(src)).then_inc(param_evac, 1)

            def param_step(q, s, use):
                if s in (0, 1):
                    if s == 0 and q:
                        act.wait_ge(bt_spilled, 16 * q)
                    for half in range(2):
                        at = (2 * s + half) * 512
                        param_take(use + half, bt_out[:, at:at + 512], 512)
                    if s == 1:
                        act.wait_ge(param_evac, use + 2)
                        act.dma_start(ssm_scr[q], bt_out).then_inc(bt_spilled, 16)
                if s == 2:
                    param_take(use, kc, 256)
                    act.wait_ge(ct_ready, q + 1)
                    act.dma_start(ssm_scr[2 * BATCHES + q], ct_out).then_inc(ct_spilled, 16)
                if s in (3, 4):
                    if s == 3 and q:
                        act.wait_ge(t_spilled, 16 * q)
                    for half in range(2):
                        b = 4 * (s - 3) + 2 * half
                        dst = t_out.rearrange("p (g b c) -> p b g c", g=16, b=LB)[:, b:b + 2]
                        param_take(use + half, dst, 512,
                                   lambda a: a.rearrange("p (b g c) -> p b g c", b=2, g=16))
                    if s == 4:
                        act.wait_ge(param_evac, use + 2)
                        act.dma_start(ssm_scr[BATCHES + q], t_out).then_inc(t_spilled, 16)

            for f in range(FF_UNITS):
                act.wait_ge(piece_done, AT["gate", f] + 1)
                if f:
                    act.wait_ge(hid_ready, f)
                act.activation(f_act, PS[:, 0, :], ACT.Silu).then_inc(gate_act, 1)
                for n in (3 * f, 3 * f + 1, 3 * f + 2) + ((3 * FF_UNITS,) if f == FF_UNITS - 1 else ()):
                    for kind, i, s, use in PLAN.get(n, []):
                        if kind == "param":
                            param_step(i, s, use)
                        elif kind == "rows":
                            act.wait_ge(piece_done, AT["mod", 2 * i + 1] + 1)
                            copy(row_late, PS[:, 2 + use % 2, :]).then_inc(param_evac, 1)
                        else:
                            param_take(use, modc[:, 4 * i:4 * i + 4], 4)

            squares(2, x_wait(2))
            root(2, 0)

            act.wait_ge(h_ready, 3 * NC)
            act.dma_start(h_scr.rearrange("(c p) t -> p c t", p=P), H).then_inc(h_stored, 16)
            act.wait_ge(h_stored, 16)
            for b in range(LB):
                act.dma_start(ust[GCH * b:GCH * (b + 1), :].rearrange("c (g k) -> c g k", g=GROUPS),
                              h_scr.rearrange("(g c) (b k) -> b c g k", c=GCH, b=LB)[b]).then_inc(u_loaded, 16)
            for q in range(BATCHES):
                act.wait_ge(piece_done, AT_BT + q + 1)
                for ri in (1, 0):
                    for g in range(2):
                        rows = slice(64 * g, 64 * g + 64)
                        copy(vbuf[rows, ri * 1024 + q * 256:ri * 1024 + (q + 1) * 256].rearrange("p (t k) -> p t k", t=BT),
                             PS[rows, 4 * ri + q, :].rearrange("p (t g k) -> p t g k", t=BT, g=2)[:, :, g, :]
                             ).then_inc(v_ready, 1)
            for q in range(BATCHES):
                act.wait_ge(piece_done, AT_T + q + 1)
                copy(ust[:, q * 512:(q + 1) * 512], PS[:, 4 + q, :]).then_inc(y_evac, 1)
            act.wait_ge(y_sum, BATCHES)
            for b in range(LB):
                act.dma_start(y_scr.rearrange("(g c) (b k) -> b c g k", c=GCH, b=LB)[b],
                              y_sb[GCH * b:GCH * (b + 1), :].rearrange("c (g k) -> c g k", g=GROUPS)).then_inc(y_stored, 16)
            act.wait_ge(y_stored, 16 * LB)
            act.dma_start(A, y_scr.rearrange("(c p) t -> p c t", p=P)).then_inc(y_loaded, 16)
            for cp in range(4):
                act.wait_ge(yd_ready, 2 * (cp + 1))
                act.activation(gT[:, 2 * cp:2 * cp + 2, :], A[:, 2 * cp:2 * cp + 2, :], ACT.Gelu_apprx_tanh).then_inc(gelu_ready, 1)
            for i in range(4):
                act.wait_ge(piece_done, AT_GLU + 2 * i + 2)
                if i >= 2:
                    act.wait_ge(x_updated, 16 + 2 * (i - 1))
                for j in range(2):
                    at = (i % 2) * 512 + j * T
                    a = act.activation(sig[:, at:at + T], PS[:, 2 + i % 2, j * T:(j + 1) * T], ACT.Sigmoid,
                                       bias=cols[:, K_GLUB + 8 + 2 * i + j:K_GLUB + 9 + 2 * i + j])
                a.then_inc(sig_ready, 1)

            squares(3, x_wait(3))
            root(3, 4)

            for m in range(4):
                act.wait_ge(htm_psum, m + 1)
                copy(h_tm[:, m * 512:(m + 1) * 512], PS[:, (6, 7, 0, 1)[m], :]).then_inc(htm_ready, 1)
            act.wait_ge(gap_ready, 1)
            act.activation(r2[5], r2[4], ACT.Exp).then_inc(pick_exp, 1)

            def take_gathered():
                copy(hgT, PS[:, 6:8, :].rearrange("p b n -> p (b n)")).then_inc(e_hg, 1)

            act.wait_ge(e_gather, 1)
            take_gathered()
            act.wait_ge(items_ready, 1)
            count = act.value_load(items[0:1, 0:1], min_val=EXPERTS, max_val=EXPERTS + EXTRA)
            with act.Fori(0, count) as it:
                for f in range(EX_UNITS):
                    act.wait_ge(piece_done, it * PER_ITEM + (PRE + EXI["gate", f] + 1))
                    if f:
                        act.wait_ge(e_hid, it * EX_UNITS + f)
                    act.activation(e_act_b, PS[:, 0, 0:256], ACT.Silu).then_inc(e_act, 1)
                act.wait_ge(e_gather, it + 2)
                take_gathered()
                act.wait_ge(piece_done, it * PER_ITEM + (PRE + PER_ITEM))
                copy(ye, PS[:, 4:6, :].rearrange("p b n -> p (b n)")).then_inc(e_y, 1)
            act.wait_ge(e_x, count * 4)
            squares(4, lambda cp: None)
            root(4, 0)
            act.wait_ge(final_ready, NC)
            act.dma_start(out, buf_h[:, :]).then_inc(out_stored, 16)
            act.wait_ge(out_stored, 16)

        @block.vector
        def _(dve):
            steps = [0]

            def link(ins):
                steps[0] += 1
                ins.then_inc(dve_step, 1)
                dve.wait_ge(dve_step, steps[0])

            def tt(o_, a, b, op):
                return dve.tensor_tensor(o_, a, b, op)

            def cmul(o_re, o_im, a_re, a_im, b_re_, b_im_, tmp):
                tt(o_re, a_re, b_re_, ALU.mult)
                link(tt(tmp, a_im, b_im_, ALU.mult))
                link(tt(o_re, o_re, tmp, ALU.subtract))
                tt(o_im, a_re, b_im_, ALU.mult)
                link(tt(tmp, a_im, b_re_, ALU.mult))
                link(tt(o_im, o_im, tmp, ALU.add))

            dve.wait_ge(cond_exp, 1)
            link(dve.tensor_scalar(att_st[:, 8:16], att_st[:, 0:8], 1.0, None, ALU.add))
            link(dve.reciprocal(att_st[:, 8:16], att_st[:, 8:16]))
            tt(cond32.rearrange("p (c n) -> p c n", c=NC), att_st[:, 8:16].unsqueeze(2).broadcast_to([P, NC, 32]),
               cols[:, K_C:K_C + 8].unsqueeze(2).broadcast_to([P, NC, 32]), ALU.mult).then_inc(cond_ready, 1)
            dve.wait_ge(dt_ready, 1)
            are, aim = cols[:, K_ARE:K_ARE + 32], cols[:, K_AIM:K_AIM + 32]
            tt(s_cols[1], are, s_cols[0], ALU.mult).then_inc(decay_arg, 1)
            tt(ang[:, 256:288], aim, s_cols[0], ALU.mult)
            dve.wait_ge(tables_loaded, 32)
            link(dve.tensor_copy(ang[:, 0:T], posi))
            link(dve.tensor_scalar(ang[:, 0:T], ang[:, 0:T], consts[:, C_INV:C_INV + 1], None, ALU.mult))
            link(dve.tensor_scalar(ang_k, ang, 1.0 / (2 * np.pi), MAGIC, ALU.mult, ALU.add))
            link(dve.tensor_scalar(ang_k, ang_k, -MAGIC, None, ALU.add))
            for part_of in two_pi_parts():
                link(dve.scalar_tensor_tensor(ang, ang_k, -part_of, ang, ALU.mult, ALU.add))
            dve.tensor_scalar(ang, ang, PI_LOW, -PI_LOW, ALU.min, ALU.max).then_inc(angle_ready, 1)

            def normalise(k):
                dve.wait_ge(rms_ready, k + 1)
                link(dve.reciprocal(stat[:, :], stat[:, :]))
                link(tt(scratch(k), resid(k), stat[:, :].unsqueeze(1).broadcast_to([P, NC, T]), ALU.mult))

            def modulate(k):
                a = acol[:, 8 * k:8 * k + 8]
                link(dve.tensor_scalar(a, part(k, 1), 1.0, None, ALU.add))
                link(tt(a, a, gain(k), ALU.mult))
                for c in range(NC):
                    dve.tensor_scalar(H[:, c, :], scratch(k)[:, c, :], a[:, c:c + 1], part(k, 0)[:, c:c + 1],
                                      ALU.mult, ALU.add).then_inc(h_ready, 1)

            def mod_take(n, to):
                dve.wait_ge(mod_cols, (to + n) // 4)
                tt(modc[:, to:to + n], PS[:, 7, to:to + n], mod_bT[:, to:to + n], ALU.add).then_inc(mod_taken, 1)

            normalise(0)
            mod_take(16, 0)
            dve.wait_ge(mod_taken, 1)
            modulate(0)

            dve.wait_ge(sines_ready, 2)
            link(tt(cosF, sin_h, sin_h, ALU.mult))
            link(dve.tensor_scalar(cosF, cosF, -2.0, 1.0, ALU.mult, ALU.add))

            cos_a, sin_a = cosF[:, 256:288], sinF[:, 256:288]
            (dt_, _, mag, ab_re, ab_im, nr, den, t1, f_re, f_im, w_re, w_im, v_re, v_im) = s_cols[:14]
            dve.wait_ge(mag_ready, 1)
            tt(ab_re, mag, cos_a, ALU.mult)
            link(tt(ab_im, mag, sin_a, ALU.mult))
            dve.tensor_scalar(nr, ab_re, -1.0, None, ALU.add)
            tt(den, are, are, ALU.mult)
            link(tt(t1, aim, aim, ALU.mult))
            link(tt(den, den, t1, ALU.add))
            link(dve.reciprocal(den, den))
            tt(f_re, nr, are, ALU.mult)
            link(tt(t1, ab_im, aim, ALU.mult))
            link(tt(f_re, f_re, t1, ALU.add))
            tt(f_re, f_re, den, ALU.mult)
            tt(f_im, ab_im, are, ALU.mult)
            link(tt(t1, nr, aim, ALU.mult))
            link(tt(f_im, f_im, t1, ALU.subtract))
            link(tt(f_im, f_im, den, ALU.mult))

            def tmp3(n):
                return sco[:, 0:TILES * n].rearrange("p (t n) -> p t n", n=n)

            def wide(a, n):
                return a.unsqueeze(2).broadcast_to([P, TILES, n])

            dve.wait_ge(ssm_loaded, 16)
            cmul(bb_re, bb_im, wide(f_re, GCH), wide(f_im, GCH), b_re, b_im, tmp3(GCH))
            dve.tensor_copy(fp_re[:, :, 0], ab_re)
            link(dve.tensor_copy(fp_im[:, :, 0], ab_im))
            for n in (1, 2, 4):
                cmul(fp_re[:, :, n:2 * n], fp_im[:, :, n:2 * n], fp_re[:, :, 0:n], fp_im[:, :, 0:n],
                     wide(fp_re[:, :, n - 1], n), wide(fp_im[:, :, n - 1], n), tmp3(n))
            dve.tensor_copy(cond_late, cond32).then_inc(cond_moved, 1)
            dve.tensor_copy(s_cols[14], aim).then_inc(powers_ready, 1)
            cmul(w_re, w_im, cos_a, sin_a, cos_a, sin_a, t1)
            cmul(v_re, v_im, w_re, w_im, w_re, w_im, t1)
            cmul(w_re, w_im, v_re, v_im, v_re, v_im, t1)
            dve.memset(ph_re[:, :, 0:1], 1.0)
            dve.memset(ph_im[:, :, 0:1], 0.0)
            dve.tensor_copy(ph_re[:, :, 1], w_re)
            link(dve.tensor_copy(ph_im[:, :, 1], w_im))
            ws = [(w_re, w_im), (v_re, v_im)]
            for lev, n in enumerate((2, 4, 8, 16)):
                (p_re, p_im), (q_re, q_im) = ws[lev % 2], ws[1 - lev % 2]
                cmul(q_re, q_im, p_re, p_im, p_re, p_im, t1)
                cmul(ph_re[:, :, n:2 * n], ph_im[:, :, n:2 * n], ph_re[:, :, 0:n], ph_im[:, :, 0:n],
                     wide(q_re, n), wide(q_im, n), tmp3(n))
            link(tt(m8[:, :], mag, mag, ALU.mult))
            link(tt(m8[:, :], m8[:, :], m8[:, :], ALU.mult))
            link(tt(m8[:, :], m8[:, :], m8[:, :], ALU.mult))

            def rope(s):
                dve.wait_ge(rope_psum, s + 1)
                if s:
                    dve.wait_ge(rope_ready, s)
                rows = (qT, kT)[s // 2][:, (s % 2) * 512:(s % 2 + 1) * 512].rearrange("p (c t) -> p c t", c=2)
                turned = rtmp.rearrange("p (c t) -> p c t", c=2)
                tt(turned, PS[:, 3 + s % 2, :].rearrange("p (c t) -> p c t", c=2),
                   sinF[:, 0:T].unsqueeze(1).broadcast_to([P, 2, T]), ALU.mult)
                link(tt(rows, rows, cosF[:, 0:T].unsqueeze(1).broadcast_to([P, 2, T]), ALU.mult))
                tt(rows, rows, turned, ALU.add).then_inc(rope_ready, 1)

            for s in range(4):
                rope(s)
            dve.wait_ge(u_padded, 1)
            for w in (8, 9):
                dve.wait_ge(piece_done, AT["in", w] + 1)
                dve.wait_ge(proj_act, 7 + w - 8)
                rows = ub[:, 2 * (w - 8):2 * (w - 8) + 2, 2:T + 2]
                tt(rows, rows, PS[:, 1 + w % 2, :].rearrange("p (c t) -> p c t", c=2), ALU.mult).then_inc(proj_dve, 1)

            def mask(h):
                dve.wait_ge(scores_ready, h + 1)
                if h >= 2:
                    dve.wait_ge(pt_psum, h - 1)
                s = sco[:, (h % 2) * 384:(h % 2 + 1) * 384]
                bank = 3 + h % 2
                mx = att_st[:, 48 + 2 * (h % 2):50 + 2 * (h % 2)]
                link(tt(s, PS[:, bank, 0:384], att_bias, ALU.add))
                dve.tensor_reduce(mx[:, 0:1], s[:, 0:128], AX.X, ALU.max).then_inc(masked_ready, 1)
                link(dve.tensor_reduce(mx[:, 1:2], s[:, 128:384], AX.X, ALU.max))
                dve.tensor_scalar(att_st[:, 16 + 2 * h:18 + 2 * h], mx, -0.125, None, ALU.mult).then_inc(negmax_ready, 1)

            def scale(h):
                dve.wait_ge(exp_ready, h + 1)
                s = sco[:, (h % 2) * 384:(h % 2 + 1) * 384]
                l = att_st[:, 32 + 2 * h:34 + 2 * h]
                link(dve.reciprocal(l, l))
                dve.tensor_scalar(s[:, 0:128], s[:, 0:128], l[:, 0:1], None, ALU.mult)
                dve.tensor_scalar(s[:, 128:384], s[:, 128:384], l[:, 1:2], None, ALU.mult).then_inc(probs_ready, 1)

            def head_pair(j):
                dve.wait_ge(pv_ready, 2 * j + 2)
                dve.tensor_copy(H[:, j, :], PS[:, 1 + j % 2, 0:T]).then_inc(attn_out, 1)

            def conv(c):
                k0 = K_CONV + c
                if c == 0:
                    dve.wait_ge(proj_dve, 2)
                    dve.wait_ge(proj_act, 10)
                y = H[:, 4 + c, :]
                link(dve.tensor_scalar(y, ub[:, c, 0:T], cols[:, k0:k0 + 1], None, ALU.mult))
                link(dve.scalar_tensor_tensor(y, ub[:, c, 1:T + 1], cols[:, k0 + 4:k0 + 5], y, ALU.mult, ALU.add))
                link(dve.scalar_tensor_tensor(y, ub[:, c, 2:T + 2], cols[:, k0 + 8:k0 + 9], y, ALU.mult, ALU.add))
                tt(y, y, bg[:, c * T:(c + 1) * T], ALU.mult).then_inc(conv_out, 1)

            mask(0)
            for h in range(HEADS):
                if h + 1 < HEADS:
                    mask(h + 1)
                if h < 4:
                    conv(h)
                scale(h)
                if h >= 3 and h % 2:
                    head_pair((h - 3) // 2)
            head_pair(3)

            def residual(k, ch, src):
                return dve.scalar_tensor_tensor(resid(k)[:, ch, :], src, part(k, 2)[:, ch:ch + 1], resid(k)[:, ch, :],
                                                ALU.mult, ALU.add)

            mod_take(24, 16)
            dve.wait_ge(mod_taken, 2)
            for w in range(W_OUT):
                dve.wait_ge(piece_done, AT["out", w] + 1)
                for j in range(2):
                    residual(0, 2 * w + j, PS[:, 3 + w % 2, j * T:(j + 1) * T]).then_inc(x_updated, 1)
            normalise(1)
            modulate(1)
            mod_take(8, 40)

            def block_inputs(q):
                if q == 0:
                    dve.wait_ge(reversed_ready, 1)
                else:
                    dve.wait_ge(param_psum, psum_count(USE["param", q - 1, 2]))
                ts = slice(BT * q, BT * (q + 1))

                def v4(a):
                    return a.rearrange("p (t b c) -> p t b c", t=BT, b=LB)

                o_re, o_im, tmp = v4(bsm[:, 0:1024]), v4(bsm[:, 1024:2048]), v4(buf_b[:, 0:1024])
                pr, pi = [a[:, ts, :].unsqueeze(3).broadcast_to([P, BT, LB, GCH]) for a in (rp_re, rp_im)]
                br, bi = [a[:, ts, :].unsqueeze(2).broadcast_to([P, BT, LB, GCH]) for a in (bb_re, bb_im)]
                tt(o_re, pr, br, ALU.mult)
                link(tt(tmp, pi, bi, ALU.mult))
                link(tt(o_re, o_re, tmp, ALU.subtract))
                tt(o_im, pr, bi, ALU.mult)
                link(tt(tmp, pi, br, ALU.mult))
                tt(o_im, o_im, tmp, ALU.add).then_inc(bsm_ready, 1)

            for f in range(FF_UNITS):
                dve.wait_ge(piece_done, AT["up", f] + 1)
                dve.wait_ge(gate_act, f + 1)
                if f >= 2:
                    dve.wait_ge(piece_done, AT["down", f - 2] + 1)
                tt(f_hid[:, (f % 2) * 512:(f % 2 + 1) * 512], f_act, PS[:, 1, :], ALU.mult).then_inc(hid_ready, 1)
                if f == 0:
                    block_inputs(0)
                for q in range(1, BATCHES):
                    if (5 + 7 * (q - 1) + 2) // 3 + 1 == f:
                        block_inputs(q)

            dve.wait_ge(piece_done, DENSE)
            dve.wait_ge(ct_ready, BATCHES)
            dve.wait_ge(bsm_ready, BATCHES)
            for n in range(NC):
                def blocked(a):
                    return a.rearrange("p (k b) -> p b k", b=LB)
                dve.scalar_tensor_tensor(B[:, n, :].rearrange("p (b k) -> p b k", b=LB),
                                         blocked(PS[:, 4 + n // 2, (n % 2) * T:(n % 2 + 1) * T]),
                                         part(1, 2)[:, n:n + 1], blocked(A[:, n, :]), ALU.mult, ALU.add).then_inc(x_updated, 1)
            dve.wait_ge(mod_taken, 3)
            dve.wait_ge(param_evac, USE["turn", MOD_GROUPS - 1, 0] + 1)
            link(tt(modc[:, 48:96], modc[:, 48:96], mod_bT[:, 48:96], ALU.add))
            normalise(2)
            modulate(2)

            dtab = pows[:, 0:1024].rearrange("p (t k) -> p t k", k=KB)
            link(dve.tensor_copy(dtab, wide(m8[:, :], KB)))
            link(dve.memset(dtab[:, :, 0:1], 0.0))
            flat_re, flat_im = phasor[:, 0:1024], phasor[:, 1024:2048]
            vr, vi, zr, zi = vbuf[:, 0:1024], vbuf[:, 1024:2048], zbuf[:, 0:1024], zbuf[:, 1024:2048]
            ta, xr = buf_a[:, 0:1024], buf_a[:, 1024:2048]
            dve.wait_ge(v_ready, 4 * BATCHES)
            tt(zr, vr, flat_re, ALU.mult)
            link(tt(ta, vi, flat_im, ALU.mult))
            link(tt(zr, zr, ta, ALU.add))
            link(dve.tensor_tensor_scan(xr, pows[:, 0:1024], zr, 0.0, ALU.mult, ALU.add))
            dve.wait_ge(z_im_ready, 1)
            dve.tensor_tensor_scan(vr, pows[:, 0:1024], zi, 0.0, ALU.mult, ALU.add).then_inc(scan_ready, 1)
            dve.wait_ge(scan_ready, 1)
            tt(zr, xr, flat_re, ALU.mult)
            link(tt(ta, vr, flat_im, ALU.mult))
            dve.wait_ge(xz_zeroed, 1)
            x4 = xz.rearrange("p (r t g k) -> p r t g k", r=2, t=TILES, g=2)
            for g in range(2):
                rows = slice(64 * g, 64 * g + 64)
                tt(x4[rows, 0, :, g, 1:KB], zr.rearrange("p (t k) -> p t k", k=KB)[rows, :, 0:KB - 1],
                   ta.rearrange("p (t k) -> p t k", k=KB)[rows, :, 0:KB - 1], ALU.subtract).then_inc(xs_re, 1)

            for q in range(BATCHES):
                dve.wait_ge(piece_done, AT_CT + q + 1)
                dve.wait_ge(y_evac, q + 1)
                tt(y_sb[:, q * 512:(q + 1) * 512], PS[:, q, :], ust[:, q * 512:(q + 1) * 512], ALU.add).then_inc(y_sum, 1)
            dve.wait_ge(y_loaded, 16)
            for c in range(NC):
                dve.scalar_tensor_tensor(A[:, c, :], H[:, c, :], cols[:, K_D + c:K_D + c + 1], A[:, c, :],
                                         ALU.mult, ALU.add).then_inc(yd_ready, 1)
            for i in range(4):
                dve.wait_ge(piece_done, AT_GLU + 2 * i + 1)
                dve.wait_ge(sig_ready, i + 1)
                for j in range(2):
                    s = sig[:, (i % 2) * 512 + j * T:(i % 2) * 512 + (j + 1) * T]
                    bias = cols[:, K_GLUB + 2 * i + j:K_GLUB + 2 * i + j + 1]
                    link(dve.scalar_tensor_tensor(s, PS[:, i % 2, j * T:(j + 1) * T], bias, s, ALU.add, ALU.mult))
                    residual(2, 2 * i + j, s).then_inc(x_updated, 1)
            normalise(3)
            modulate(3)

            def v2(a):
                return a.rearrange("p (t e) -> p t e", e=EXPERTS)

            def wide2(a):
                return a.unsqueeze(2).broadcast_to([P, 2, EXPERTS])

            logit, eq, first, rest, second, gates, M, place = r[0], r[1], r[3], r[4], r[5], r[6], r[7], r[8]

            def best(src, onehot, mx, at):
                link(dve.tensor_reduce(mx, v2(src), AX.X, ALU.max))
                link(tt(v2(eq), v2(src), wide2(mx), ALU.is_equal))
                link(tt(eq, eq, rev, ALU.mult))
                link(dve.tensor_reduce(at, v2(eq), AX.X, ALU.max))
                link(tt(v2(onehot), v2(rev), wide2(at), ALU.is_equal))

            dve.wait_ge(logits_ready, 1)
            link(tt(logit, PS[:, 5, 0:16], cols[:, K_RB:K_RB + 16], ALU.add))
            best(logit, first, r2[0], r2[1])
            link(dve.scalar_tensor_tensor(rest, first, -3e38, logit, ALU.mult, ALU.add))
            best(rest, second, r2[2], r2[3])
            tt(M, first, second, ALU.add).then_inc(picked_ready, 1)
            tt(r2[4], r2[2], r2[0], ALU.subtract).then_inc(gap_ready, 1)
            dve.wait_ge(pick_exp, 1)
            link(dve.tensor_scalar(r2[6], r2[5], 1.0, None, ALU.add))
            link(dve.reciprocal(r2[6], r2[6]))
            link(tt(r2[7], r2[5], r2[6], ALU.mult))
            tt(v2(gates), v2(first), wide2(r2[6]), ALU.mult)
            link(tt(v2(eq), v2(second), wide2(r2[7]), ALU.mult))
            link(tt(gates, gates, eq, ALU.add))
            dve.wait_ge(pos_ready, 1)
            dve.wait_ge(picked_ready, 1)
            link(dve.scalar_tensor_tensor(place, PS[:, 2, 0:16], 1.0, M, ALU.add, ALU.mult))

            def by_item(a):
                return a[:, 0:16].rearrange("p (e t) -> p t e", t=2)

            dve.tensor_scalar(by_item(posx), v2(place), -1.0, None, ALU.add)
            dve.tensor_copy(by_item(gx), v2(gates))
            dve.memset(posx[:, 22:24], -1.0)
            later, over, upto, pick, prod = r[2], r[9][:, 0:8], r[9][:, 8:16], r[10][:, 0:8], r[11]
            link(dve.tensor_scalar(later, place, -1.0 - SLOT, None, ALU.add))
            dve.tensor_scalar(few[:, 0:EXPERTS], PS[:, 2, 16:24], float(HALF), None, ALU.is_le)
            link(dve.tensor_scalar(over, PS[:, 2, 16:24], float(SLOT), None, ALU.is_gt))
            link(dve.tensor_tensor_scan(upto, ones[:, 0:8], over, 0.0, ALU.mult, ALU.add))
            link(dve.tensor_scalar(items[:, 0:1], upto[:, 7:8], float(EXPERTS), None, ALU.add))
            for n in range(EXTRA):
                both = pick.unsqueeze(1).broadcast_to([P, 2, EXPERTS])
                at = 16 + 2 * n
                link(dve.scalar_tensor_tensor(pick, upto, float(n + 1), over, ALU.is_equal, ALU.mult))
                link(tt(v2(prod), v2(later), both, ALU.mult))
                link(dve.tensor_reduce(posx[:, at:at + 2], v2(prod), AX.X, ALU.add))
                link(tt(v2(prod), v2(gates), both, ALU.mult))
                link(dve.tensor_reduce(gx[:, at:at + 2], v2(prod), AX.X, ALU.add))
                link(tt(prod[:, 0:8], pick, PS[:, 2, 16:24], ALU.mult))
                link(dve.tensor_reduce(r2[1][:, 0:1], prod[:, 0:8], AX.X, ALU.add))
                link(dve.tensor_scalar(few[:, EXPERTS + n:EXPERTS + n + 1], r2[1][:, 0:1], float(SLOT + HALF), None,
                                       ALU.is_le))
                link(tt(prod[:, 0:8], pick, rev[:, 0:8], ALU.mult))
                link(dve.tensor_reduce(r2[1][:, 0:1], prod[:, 0:8], AX.X, ALU.add))
                link(dve.tensor_scalar(r2[1][:, 0:1], r2[1][:, 0:1], -1.0, float(EXPERTS), ALU.mult, ALU.add))
                s = dve.tensor_scalar(items[:, n + 1:n + 2], r2[1][:, 0:1], float(EXPERTS - 1), None, ALU.min)
                link(s)
            dve.memset(fold[:, 0:HALF], 0.0)
            dve.memset(fold[:, HALF:SLOT], -float(HALF))
            dve.tensor_copy(items[:, 1 + EXTRA:], few).then_inc(items_ready, 1)
            for t_ in range(2):
                s = dve.tensor_scalar(sel[:, t_ * SLOT:(t_ + 1) * SLOT], iota, posx[:, t_:t_ + 1], None, ALU.is_equal)
            s.then_inc(e_sel, 1)

            dve.wait_ge(items_ready, 1)
            count = dve.value_load(items[0:1, 0:1], min_val=EXPERTS, max_val=EXPERTS + EXTRA)
            with dve.Fori(0, count) as it:
                def col(a, at):
                    return a[:, bass.ds(at, 1)]

                dve.scalar_tensor_tensor(iota_item, fold, col(few, it), iota, ALU.mult, ALU.add).then_inc(e_iota, 1)
                dve.wait_ge(e_iota, it + 1)
                for t_ in range(2):
                    s = dve.tensor_scalar(selg[:, t_ * SLOT:(t_ + 1) * SLOT], iota_item, col(posx, it * 2 + t_),
                                          col(gx, it * 2 + t_), ALU.is_equal, ALU.mult)
                s.then_inc(e_selg, 1)
                dve.wait_ge(e_gather, it + 1)
                for t_ in range(2):
                    s = dve.tensor_scalar(sel[:, t_ * SLOT:(t_ + 1) * SLOT], iota, col(posx, it * 2 + (t_ + 2)),
                                          None, ALU.is_equal)
                s.then_inc(e_sel, 1)
                for f in range(EX_UNITS):
                    dve.wait_ge(piece_done, it * PER_ITEM + (PRE + EXI["up", f] + 1))
                    dve.wait_ge(e_act, it * EX_UNITS + (f + 1))
                    if f >= 2:
                        dve.wait_ge(piece_done, it * PER_ITEM + (PRE + EXI["down", f - 2] + 1))
                    tt(e_hid_b[:, (f % 2) * 256:(f % 2 + 1) * 256], e_act_b, PS[:, 1, 0:256], ALU.mult).then_inc(e_hid, 1)
                    if f == 1:
                        dve.wait_ge(e_gtp, it + 1)
                        dve.tensor_copy(gt, PS[:, 2, 0:256]).then_inc(e_gt, 1)
                for m in range(4):
                    dve.wait_ge(e_scat, it * 4 + (m + 1))
                    for j in range(2):
                        s = residual(3, 2 * m + j, PS[:, (2, 3, 6, 7)[m], j * T:(j + 1) * T])
                    s.then_inc(e_x, 1)

            normalise(4)
            for c in range(NC):
                dve.tensor_scalar(H[:, c, :], A[:, c, :], gain(4)[:, c:c + 1], None, ALU.mult).then_inc(final_ready, 1)

        @block.gpsimd
        def _(pool):
            steps = [0]

            def link(ins):
                steps[0] += 1
                ins.then_inc(pool_step, 1)
                pool.wait_ge(pool_step, steps[0])

            def tt(o_, a, b, op):
                return pool.tensor_tensor(o_, a, b, op)

            pool.memset(ub[:, :, 0:2], 0.0).then_inc(u_padded, 1)
            pool.wait_ge(powers_ready, 1)
            pool.memset(rp_re[:, :, 7:8], 1.0)
            pool.memset(rp_im[:, :, 7:8], 0.0)
            for b in range(7):
                pool.tensor_copy(rp_re[:, :, b], fp_re[:, :, 6 - b])
                s = pool.tensor_copy(rp_im[:, :, b], fp_im[:, :, 6 - b])
            s.then_inc(reversed_ready, 1)

            pool.wait_ge(h_ready, 2 * NC)
            link(pool.memset(cz, 0.0))
            c4 = cz.rearrange("p (r t g c) -> p r t g c", r=2, t=BT, g=2)
            out4 = ct_out.rearrange("p (t r b c) -> p r t b c", t=BT, r=2, b=LB)
            tmp = buf_b[:, 1024:2048].rearrange("p (t b c) -> p t b c", t=BT, b=LB)
            for q in range(BATCHES):
                ts = slice(BT * q, BT * (q + 1))
                if q:
                    pool.wait_ge(param_psum, psum_count(USE["param", q - 1, 2]))
                for g in range(2):
                    rows = slice(64 * g, 64 * g + 64)
                    link(pool.tensor_copy(c4[rows, 0, :, g, :], c_re[rows, ts, :]))
                    s = pool.tensor_scalar(c4[rows, 1, :, g, :], c_im[rows, ts, :], -1.0, None, ALU.mult)
                    if g == 0:
                        link(s)
                s.then_inc(cz_ready, 1)
                pool.wait_ge(cz_ready, q + 1)
                if q:
                    pool.wait_ge(ct_spilled, 16 * q)
                pr, pi = [a[:, ts, :].unsqueeze(3).broadcast_to([P, BT, LB, GCH]) for a in (fp_re, fp_im)]
                cr, ci = [a[:, ts, :].unsqueeze(2).broadcast_to([P, BT, LB, GCH]) for a in (c_re, c_im)]
                tt(out4[:, 0], cr, pr, ALU.mult)
                link(tt(tmp, ci, pi, ALU.mult))
                link(tt(out4[:, 0], out4[:, 0], tmp, ALU.subtract))
                tt(out4[:, 1], cr, pi, ALU.mult)
                link(tt(tmp, ci, pr, ALU.mult))
                link(tt(out4[:, 1], out4[:, 1], tmp, ALU.add))
                pool.tensor_scalar(out4[:, 1], out4[:, 1], -1.0, None, ALU.mult).then_inc(ct_ready, 1)

            pool.wait_ge(h_ready, 3 * NC)
            pool.wait_ge(t_spilled, 16 * BATCHES)
            pool.memset(xz, 0.0).then_inc(xz_zeroed, 1)
            flat_re, flat_im = phasor[:, 0:1024], phasor[:, 1024:2048]
            vr, vi, zi = vbuf[:, 0:1024], vbuf[:, 1024:2048], zbuf[:, 1024:2048]
            xr, tb = buf_a[:, 1024:2048], bb[:, 0:1024]
            pool.wait_ge(v_ready, 4 * BATCHES)
            tt(zi, vi, flat_re, ALU.mult)
            link(tt(tb, vr, flat_im, ALU.mult))
            tt(zi, zi, tb, ALU.subtract).then_inc(z_im_ready, 1)
            pool.wait_ge(scan_ready, 1)
            tt(zi, xr, flat_im, ALU.mult)
            link(tt(tb, vr, flat_re, ALU.mult))
            pool.wait_ge(xz_zeroed, 1)
            x4 = xz.rearrange("p (r t g k) -> p r t g k", r=2, t=TILES, g=2)
            for g in range(2):
                rows = slice(64 * g, 64 * g + 64)
                tt(x4[rows, 1, :, g, 1:KB], zi.rearrange("p (t k) -> p t k", k=KB)[rows, :, 0:KB - 1],
                   tb.rearrange("p (t k) -> p t k", k=KB)[rows, :, 0:KB - 1], ALU.add).then_inc(xs_im, 1)
                pool.wait_ge(xs_im, g + 1)


def shape_constants():
    t = np.zeros((P, C_ALL), np.float32)
    t[:, C_ID:C_ID + P] = np.eye(P)
    rope = HEAD // 4
    for m in range(P):
        d = m % HEAD
        if d < rope // 2:
            t[m + rope // 2, C_ROT + m] = -1.0
        elif d < rope:
            t[m - rope // 2, C_ROT + m] = 1.0
        if d < rope:
            t[m, C_INV] = np.float32(500000.0) ** np.float32(-2.0 * (d % (rope // 2)) / rope)
    t[:, C_ONE:C_ONE + P] = 1.0
    t[:, C_TRI:C_TRI + P] = np.triu(np.ones((P, P)), 1)
    dist = np.arange(T)[:, None] - np.arange(T)[None, :]
    many = sum(((dist >= 0) & (dist <= w) & (dist % dil == 0)).astype(int) for w, dil in ((128, 1), (512, 4), (2048, 16)))
    bias = np.where(many > 0, 8.0 * np.log(np.maximum(many, 1)), -1e30)
    t[:, C_BIAS:C_BIAS + 128] = bias[:128, :128]
    t[:, C_BIAS + 128:C_BIAS + 384] = bias[128:, :]
    t[:, C_IOTA:C_IOTA + P] = np.arange(P)
    t[:, C_REV:C_REV + 16] = np.tile(8 - np.arange(8), 2)
    t[:, C_EPS] = EPS
    t[::32, C_QUAD] = 1.0
    return t


def kernel(x, c, positions, mod_w, mod_b, norm_mix_g, norm_ffn_g, ev_w_in, ev_conv_w, ev_w_out, ffn_w_gate, ffn_w_up,
           ffn_w_down, ssm_a_re, ssm_a_im, ssm_log_step, ssm_b_re, ssm_b_im, ssm_c_re, ssm_c_im, ssm_d, glu_w, glu_b,
           moe_router_w, moe_router_b, moe_w_gate, moe_w_up, moe_w_down, final_norm_g):
    import concourse.bacc as bacc
    from concourse.bass_utils import run_bass_kernel_spmd

    def columns(a):
        return np.asarray(a).reshape(-1, P).T

    def rows_in(w):
        w = np.asarray(w)
        return w.reshape(NC, P, w.shape[1] // FB, FB).transpose(2, 1, 0, 3).reshape(-1, P, PIECE)

    def rows_down(w):
        w = np.asarray(w)
        return w.reshape(w.shape[0] // FB, 2, P, D).transpose(0, 2, 1, 3).reshape(-1, P, PIECE)

    def states(a):
        a = np.asarray(a)
        a = a.reshape((TILES, P) + a.shape[2:])
        return np.moveaxis(a, 0, 1).reshape(P, -1)

    def units(gate, up, down):
        by = {"gate": rows_in(gate), "up": rows_in(up), "down": rows_down(down)}
        return [by[k][f:f + 1] for k, f in unit_order(len(by["gate"]))]

    by = {
        "mod": np.concatenate([rows_in(np.asarray(mod_w)[l]) for l in range(2)]),
        "in": rows_in(np.asarray(ev_w_in)[0])[[0, 1, 2, 3, 4, 5, 8, 9, 10, 11, 6, 7]],
        "out": rows_in(np.asarray(ev_w_out)[0]), "gate": rows_in(np.asarray(ffn_w_gate)[0]),
        "up": rows_in(np.asarray(ffn_w_up)[0]), "down": rows_down(np.asarray(ffn_w_down)[0]),
    }
    glu = rows_in(np.asarray(glu_w)[0])[[0, 4, 1, 5, 2, 6, 3, 7]]
    dense_stream = np.concatenate([by[k][i:i + 1] for k, i in ORDER] + [glu])
    expert_stream = np.concatenate([p for e in range(EXPERTS) for p in units(
        np.asarray(moe_w_gate)[0, e], np.asarray(moe_w_up)[0, e], np.asarray(moe_w_down)[0, e])])
    mix_g, ffn_g = np.asarray(norm_mix_g), np.asarray(norm_ffn_g)
    small = np.concatenate([
        columns(c), columns(mod_b), columns(mix_g[0]), columns(ffn_g[0]), columns(mix_g[1]), columns(ffn_g[1]),
        columns(final_norm_g), columns(np.asarray(ev_conv_w)[0]), columns(ssm_d), columns(glu_b),
        states(np.asarray(ssm_a_re)[0]), states(np.asarray(ssm_a_im)[0]),
        states(np.repeat(np.asarray(ssm_log_step)[0][:, None], STATES, 1)),
        np.broadcast_to(np.tile(np.asarray(moe_router_b)[0], 2), (P, 16)),
        np.asarray(moe_router_w)[0].reshape(NC, P, EXPERTS).transpose(1, 0, 2).reshape(P, -1)], axis=1)
    ssm_small = np.concatenate([states(np.asarray(ssm_b_re)[0]), states(np.asarray(ssm_b_im)[0]),
                                states(np.asarray(ssm_c_re)[0].transpose(0, 2, 1)),
                                states(np.asarray(ssm_c_im)[0].transpose(0, 2, 1))], axis=1)
    arrays = {
        "xt": np.asarray(x)[0].T.reshape(NC, P, T).transpose(1, 0, 2).reshape(P, -1),
        "positions": np.asarray(positions), "small": small, "consts": shape_constants(), "ssm_small": ssm_small,
        "dense_stream": dense_stream, "expert_stream": expert_stream,
    }
    arrays = {"in_" + n: np.ascontiguousarray(a) for n, a in arrays.items()}
    nc = bacc.Bacc("TRN2", target_bir_lowering=False, num_devices=1)
    args = [nc.dram_tensor(n, a.shape, mybir.dt.from_np(a.dtype), kind="ExternalInput").ap() for n, a in arrays.items()]
    h_scr = nc.dram_tensor("h_scratch", (D, T), F32, kind="Internal").ap()
    y_scr = nc.dram_tensor("y_scratch", (D, T), F32, kind="Internal").ap()
    ssm_scr = nc.dram_tensor("ssm_scratch", (SSM, P, PIECE), F32, kind="Internal").ap()
    out = nc.dram_tensor("out_t", (P, NC * T), F32, kind="ExternalOutput").ap()
    trunk_kernel(nc, *args, h_scr, y_scr, ssm_scr, out)
    res = run_bass_kernel_spmd(nc, [arrays], core_ids=[0]).results[0]["out_t"]
    return np.asarray(res).reshape(P, NC, LB, KB).transpose(3, 2, 1, 0).reshape(1, T, D)
```
